# Optimizing a Trainium2 kernel written in Bass

```python
import math
import jax, jax.numpy as jnp
from jax import lax
import numpy as np

D_MODEL = 1024
BATCH = 1
SEQ = 256
DEPTH = 2

N_MEM = 256
EPS = 1e-6
ATTN_HEADS = 8
ATTN_KV_HEADS = 2
ATTN_REP = ATTN_HEADS // ATTN_KV_HEADS
ATTN_HEAD_DIM = 64
ATTN_WIDTH = ATTN_HEADS * ATTN_HEAD_DIM
ATTN_KV_WIDTH = ATTN_KV_HEADS * ATTN_HEAD_DIM
WINDOW = 128
ATTN_BLOCK = 128
S5_WIDTH = 512
S5_GROUP = 16
S5_GROUPS = S5_WIDTH // S5_GROUP
S5_STATE = 64
S5_DT_MIN = 0.001
S5_DT_MAX = 0.1
SSD_INNER = D_MODEL
SSD_HEAD_DIM = 64
SSD_HEADS = SSD_INNER // SSD_HEAD_DIM
SSD_GROUPS = 2
SSD_STATE = 64
SSD_CONV = 4
SSD_CHUNK = 128
SSD_CONV_DIM = SSD_INNER + 2 * SSD_GROUPS * SSD_STATE
N_BRANCH = 3
IN_COLS = ATTN_WIDTH + 2 * ATTN_KV_WIDTH + S5_WIDTH + SSD_INNER + SSD_CONV_DIM + SSD_HEADS + N_BRANCH * D_MODEL
XA_HEADS = 4
XA_HEAD_DIM = 64
XA_WIDTH = XA_HEADS * XA_HEAD_DIM
PEER_HEADS = 8
PEER_KEY_DIM = 256
PEER_N_KEYS = 128
PEER_N_EXPERTS = PEER_N_KEYS * PEER_N_KEYS
PEER_TOPK = 16
PEER_TOKEN_BLOCK = 128

kernel_name = 'hybrid_gated_swa_s5_ssd_peer_block'

def rmsnorm(x, g):
    xf = x.astype(jnp.float32)
    y = xf * lax.rsqrt(jnp.mean(xf * xf, axis=-1, keepdims=True) + EPS)
    return (y * g.astype(jnp.float32)).astype(x.dtype)

def alibi_slopes(n):
    return 2.0 ** (-8.0 * (jnp.arange(n, dtype=jnp.float32) + 1.0) / n)

def _split_in_proj(proj):
    sizes = (ATTN_WIDTH, ATTN_KV_WIDTH, ATTN_KV_WIDTH, S5_WIDTH, SSD_INNER, SSD_CONV_DIM, SSD_HEADS)
    offs = []
    acc = 0
    for s in sizes:
        acc += s
        offs.append(acc)
    return jnp.split(proj, offs, axis=-1)

def sliding_window_attention(q, k, v, sinks):
    b, l, _ = q.shape
    nb = l // ATTN_BLOCK
    qb = q.reshape(b, nb, ATTN_BLOCK, ATTN_KV_HEADS, ATTN_REP, ATTN_HEAD_DIM)
    kb = k.reshape(b, nb, ATTN_BLOCK, ATTN_KV_HEADS, ATTN_HEAD_DIM)
    vb = v.reshape(b, nb, ATTN_BLOCK, ATTN_KV_HEADS, ATTN_HEAD_DIM)

    def with_prev(t):
        prev = jnp.concatenate([jnp.zeros_like(t[:, :1]), t[:, :-1]], axis=1)
        return jnp.concatenate([prev, t], axis=2)

    kk = with_prev(kb)
    vv = with_prev(vb)
    s = jnp.einsum('bnqgrd,bnkgd->bgrnqk', qb, kk).astype(jnp.float32) * (ATTN_HEAD_DIM ** -0.5)
    qi = jnp.arange(ATTN_BLOCK)[:, None]
    kj = jnp.arange(2 * ATTN_BLOCK)[None, :]
    dist = qi - kj + ATTN_BLOCK
    blk = jnp.arange(nb)[:, None, None]
    valid = (dist >= 0) & (dist < WINDOW) & ((blk > 0) | (kj >= ATTN_BLOCK))
    slopes = alibi_slopes(ATTN_HEADS).reshape(ATTN_KV_HEADS, ATTN_REP)
    s = s - slopes[:, :, None, None, None] * dist.astype(jnp.float32)
    s = jnp.where(valid, s, -jnp.inf)
    sink = jnp.broadcast_to(sinks.astype(jnp.float32).reshape(1, ATTN_KV_HEADS, ATTN_REP, 1, 1, 1), s.shape[:-1] + (1,))
    p = jax.nn.softmax(jnp.concatenate([s, sink], axis=-1), axis=-1)[..., :-1]
    o = jnp.einsum('bgrnqk,bnkgd->bnqgrd', p.astype(q.dtype), vv)
    return o.reshape(b, l, ATTN_WIDTH)

def _complex_linear_combine(e1, e2):
    a1r, a1i, b1r, b1i = e1
    a2r, a2i, b2r, b2i = e2
    return (a2r * a1r - a2i * a1i,
            a2r * a1i + a2i * a1r,
            a2r * b1r - a2i * b1i + b2r,
            a2r * b1i + a2i * b1r + b2i)

def s5_mixer(u, lam_re, lam_im, log_dt, b_re, b_im, c_re, c_im, d):
    bsz, l, _ = u.shape
    f32 = jnp.float32
    uf = u.astype(f32).reshape(bsz, l, S5_GROUPS, S5_GROUP)
    dt = jnp.exp(log_dt.astype(f32))[:, None]
    lr = lam_re.astype(f32)
    li = lam_im.astype(f32)
    mag = jnp.exp(lr * dt)
    ar = mag * jnp.cos(li * dt)
    ai = mag * jnp.sin(li * dt)
    den = lr * lr + li * li
    nr = ar - 1.0
    wr = (nr * lr + ai * li) / den
    wi = (ai * lr - nr * li) / den
    br_, bi_ = b_re.astype(f32), b_im.astype(f32)
    bbr = wr[..., None] * br_ - wi[..., None] * bi_
    bbi = wr[..., None] * bi_ + wi[..., None] * br_
    bu_r = jnp.einsum('blgi,gpi->blgp', uf, bbr)
    bu_i = jnp.einsum('blgi,gpi->blgp', uf, bbi)
    a_r = jnp.broadcast_to(ar, bu_r.shape)
    a_i = jnp.broadcast_to(ai, bu_i.shape)
    _, _, xr, xi = lax.associative_scan(_complex_linear_combine, (a_r, a_i, bu_r, bu_i), axis=1)
    y = jnp.einsum('blgp,gip->blgi', xr, c_re.astype(f32)) - jnp.einsum('blgp,gip->blgi', xi, c_im.astype(f32))
    y = y.reshape(bsz, l, S5_WIDTH) + d.astype(f32) * u.astype(f32)
    return y.astype(u.dtype)

def segsum(a):
    t = a.shape[-1]
    cs = jnp.cumsum(a, axis=-1)
    diff = cs[..., :, None] - cs[..., None, :]
    mask = jnp.tril(jnp.ones((t, t), dtype=bool))
    return jnp.where(mask, diff, -jnp.inf)

def ssd_scan(x, dt, a, bm, cm):
    b, l, h, p = x.shape
    n = bm.shape[-1]
    c = l // SSD_CHUNK
    xr = (x * dt[..., None]).reshape(b, c, SSD_CHUNK, h, p)
    br = bm.reshape(b, c, SSD_CHUNK, h, n)
    cr = cm.reshape(b, c, SSD_CHUNK, h, n)
    ad = (dt * a).reshape(b, c, SSD_CHUNK, h).transpose(0, 3, 1, 2)
    a_cs = jnp.cumsum(ad, axis=-1)
    lmat = jnp.exp(segsum(ad))
    scores = jnp.einsum('bclhn,bcshn->bhcls', cr, br) * lmat
    y_diag = jnp.einsum('bhcls,bcshp->bclhp', scores, xr)
    decay_states = jnp.exp(a_cs[..., -1:] - a_cs)
    states = jnp.einsum('bclhn,bhcl,bclhp->bchpn', br, decay_states, xr)
    states = jnp.concatenate([jnp.zeros_like(states[:, :1]), states], axis=1)
    chunk_decay = jnp.exp(segsum(jnp.pad(a_cs[..., -1], ((0, 0), (0, 0), (1, 0)))))
    states = jnp.einsum('bhzc,bchpn->bzhpn', chunk_decay, states)[:, :-1]
    y_off = jnp.einsum('bclhn,bchpn,bhcl->bclhp', cr, states, jnp.exp(a_cs))
    return (y_diag + y_off).reshape(b, l, h, p)

def ssd_mixer(z, xbc, dt_raw, conv_w, conv_b, dt_bias, a_log, d, norm_w):
    b, l, _ = xbc.shape
    f32 = jnp.float32
    xbc = lax.conv_general_dilated(xbc, conv_w[:, None, :], window_strides=(1,), padding=[(SSD_CONV - 1, 0)],
                                   dimension_numbers=('NWC', 'WIO', 'NWC'), feature_group_count=SSD_CONV_DIM) + conv_b
    xbc = jax.nn.silu(xbc)
    xs, bm, cm = jnp.split(xbc, [SSD_INNER, SSD_INNER + SSD_GROUPS * SSD_STATE], axis=-1)
    xs = xs.reshape(b, l, SSD_HEADS, SSD_HEAD_DIM).astype(f32)
    rep = SSD_HEADS // SSD_GROUPS
    bm = jnp.repeat(bm.reshape(b, l, SSD_GROUPS, SSD_STATE), rep, axis=2).astype(f32)
    cm = jnp.repeat(cm.reshape(b, l, SSD_GROUPS, SSD_STATE), rep, axis=2).astype(f32)
    dt = jax.nn.softplus(dt_raw.astype(f32) + dt_bias.astype(f32))
    a = -jnp.exp(a_log.astype(f32))
    y = ssd_scan(xs, dt, a, bm, cm) + d.astype(f32)[:, None] * xs
    y = y.reshape(b, l, SSD_INNER).astype(z.dtype)
    return rmsnorm(y * jax.nn.silu(z), norm_w)

def memory_cross_attention(h, mem, wq, wkv, wo):
    b, l, _ = h.shape
    m = mem.shape[1]
    q = (h @ wq).reshape(b, l, XA_HEADS, XA_HEAD_DIM)
    k, v = jnp.split(mem @ wkv, 2, axis=-1)
    k = k.reshape(b, m, XA_HEADS, XA_HEAD_DIM)
    v = v.reshape(b, m, XA_HEADS, XA_HEAD_DIM)
    s = jnp.einsum('blhd,bmhd->bhlm', q, k).astype(jnp.float32) * (XA_HEAD_DIM ** -0.5)
    p = jax.nn.softmax(s, axis=-1).astype(h.dtype)
    o = jnp.einsum('bhlm,bmhd->blhd', p, v).reshape(b, l, XA_WIDTH)
    return o @ wo

def peer_ffn(h, wq, k1, k2, u, v):
    b, l, dm = h.shape
    tokens = h.reshape(-1, PEER_TOKEN_BLOCK, dm)
    half = PEER_KEY_DIM // 2

    def block(xb):
        t = xb.shape[0]
        q = (xb @ wq).reshape(t, PEER_HEADS, 2, half)
        s1 = jnp.einsum('thd,kd->thk', q[:, :, 0], k1).astype(jnp.float32)
        s2 = jnp.einsum('thd,kd->thk', q[:, :, 1], k2).astype(jnp.float32)
        v1, i1 = lax.top_k(s1, PEER_TOPK)
        v2, i2 = lax.top_k(s2, PEER_TOPK)
        cand = (v1[..., :, None] + v2[..., None, :]).reshape(t, PEER_HEADS, PEER_TOPK * PEER_TOPK)
        cidx = (i1[..., :, None] * PEER_N_KEYS + i2[..., None, :]).reshape(t, PEER_HEADS, PEER_TOPK * PEER_TOPK)
        top, pos = lax.top_k(cand, PEER_TOPK)
        eidx = jnp.take_along_axis(cidx, pos, axis=-1)
        g = jax.nn.softmax(top, axis=-1)
        ue = jnp.take(u, eidx, axis=0)
        ve = jnp.take(v, eidx, axis=0)
        act = jax.nn.gelu(jnp.einsum('thkd,td->thk', ue, xb))
        return jnp.einsum('thk,thkd->td', (g * act.astype(jnp.float32)).astype(xb.dtype), ve)

    out = lax.map(block, tokens)
    return out.reshape(b, l, dm)

def setup_inputs(seed: int = 0) -> dict:
    key = jax.random.key(seed)
    ks = iter(jax.random.split(key, 40))
    f32 = jnp.float32
    L = DEPTH

    def nrm(shape, scale):
        return scale * jax.random.normal(next(ks), shape, f32)

    def gain(shape):
        return 1.0 + nrm(shape, 0.02)

    x = nrm((BATCH, SEQ, D_MODEL), 1.0)
    mem = nrm((BATCH, N_MEM, D_MODEL), 1.0)
    norm_mix = gain((L, D_MODEL))
    w_in = nrm((L, D_MODEL, IN_COLS), D_MODEL ** -0.5)
    attn_sinks = nrm((L, ATTN_HEADS), 1.0)
    s5_lambda_re = -0.5 + nrm((L, S5_GROUPS, S5_STATE), 0.01)
    s5_lambda_im = math.pi * jnp.arange(S5_STATE, dtype=f32) + nrm((L, S5_GROUPS, S5_STATE), 0.01)
    s5_log_dt = jax.random.uniform(next(ks), (L, S5_GROUPS), f32, math.log(S5_DT_MIN), math.log(S5_DT_MAX))
    s5_b_re = nrm((L, S5_GROUPS, S5_STATE, S5_GROUP), (2 * S5_GROUP) ** -0.5)
    s5_b_im = nrm((L, S5_GROUPS, S5_STATE, S5_GROUP), (2 * S5_GROUP) ** -0.5)
    s5_c_re = nrm((L, S5_GROUPS, S5_GROUP, S5_STATE), (2 * S5_STATE) ** -0.5)
    s5_c_im = nrm((L, S5_GROUPS, S5_GROUP, S5_STATE), (2 * S5_STATE) ** -0.5)
    s5_d = nrm((L, S5_WIDTH), 1.0)
    s5_glu_a = nrm((L, S5_WIDTH, D_MODEL), S5_WIDTH ** -0.5)
    s5_glu_b = nrm((L, S5_WIDTH, D_MODEL), S5_WIDTH ** -0.5)
    ssd_conv_w = nrm((L, SSD_CONV, SSD_CONV_DIM), SSD_CONV ** -0.5)
    ssd_conv_b = nrm((L, SSD_CONV_DIM), 0.02)
    dt0 = jnp.exp(jax.random.uniform(next(ks), (L, SSD_HEADS), f32, math.log(0.001), math.log(0.1)))
    ssd_dt_bias = dt0 + jnp.log(-jnp.expm1(-dt0))
    ssd_a_log = jnp.log(jax.random.uniform(next(ks), (L, SSD_HEADS), f32, 1.0, 16.0))
    ssd_d = gain((L, SSD_HEADS))
    ssd_norm = gain((L, SSD_INNER))
    w_attn_out = nrm((L, ATTN_WIDTH, D_MODEL), ATTN_WIDTH ** -0.5)
    w_ssd_out = nrm((L, SSD_INNER, D_MODEL), SSD_INNER ** -0.5)
    w_o = nrm((L, D_MODEL, D_MODEL), D_MODEL ** -0.5)
    norm_xattn = gain((L, D_MODEL))
    norm_mem = gain((L, D_MODEL))
    xa_wq = nrm((L, D_MODEL, XA_WIDTH), D_MODEL ** -0.5)
    xa_wkv = nrm((L, D_MODEL, 2 * XA_WIDTH), D_MODEL ** -0.5)
    xa_wo = nrm((L, XA_WIDTH, D_MODEL), XA_WIDTH ** -0.5)
    norm_ffn = gain((L, D_MODEL))
    peer_wq = nrm((L, D_MODEL, PEER_HEADS * PEER_KEY_DIM), D_MODEL ** -0.5)
    peer_k1 = nrm((L, PEER_N_KEYS, PEER_KEY_DIM // 2), (PEER_KEY_DIM // 2) ** -0.5)
    peer_k2 = nrm((L, PEER_N_KEYS, PEER_KEY_DIM // 2), (PEER_KEY_DIM // 2) ** -0.5)
    peer_u = nrm((L, PEER_N_EXPERTS, D_MODEL), D_MODEL ** -0.5)
    peer_v = nrm((L, PEER_N_EXPERTS, D_MODEL), (PEER_HEADS * PEER_TOPK) ** -0.5 * 4.0)
    norm_final = gain((D_MODEL,))
    return {'x': x, 'mem': mem, 'norm_mix': norm_mix, 'w_in': w_in, 'attn_sinks': attn_sinks,
            's5_lambda_re': s5_lambda_re, 's5_lambda_im': s5_lambda_im, 's5_log_dt': s5_log_dt,
            's5_b_re': s5_b_re, 's5_b_im': s5_b_im, 's5_c_re': s5_c_re, 's5_c_im': s5_c_im, 's5_d': s5_d,
            's5_glu_a': s5_glu_a, 's5_glu_b': s5_glu_b, 'ssd_conv_w': ssd_conv_w, 'ssd_conv_b': ssd_conv_b,
            'ssd_dt_bias': ssd_dt_bias, 'ssd_a_log': ssd_a_log, 'ssd_d': ssd_d, 'ssd_norm': ssd_norm,
            'w_attn_out': w_attn_out, 'w_ssd_out': w_ssd_out, 'w_o': w_o, 'norm_xattn': norm_xattn,
            'norm_mem': norm_mem, 'xa_wq': xa_wq, 'xa_wkv': xa_wkv, 'xa_wo': xa_wo, 'norm_ffn': norm_ffn,
            'peer_wq': peer_wq, 'peer_k1': peer_k1, 'peer_k2': peer_k2, 'peer_u': peer_u, 'peer_v': peer_v,
            'norm_final': norm_final}

def reference(x, mem, norm_mix, w_in, attn_sinks, s5_lambda_re, s5_lambda_im, s5_log_dt, s5_b_re, s5_b_im,
              s5_c_re, s5_c_im, s5_d, s5_glu_a, s5_glu_b, ssd_conv_w, ssd_conv_b, ssd_dt_bias, ssd_a_log, ssd_d,
              ssd_norm, w_attn_out, w_ssd_out, w_o, norm_xattn, norm_mem, xa_wq, xa_wkv, xa_wo, norm_ffn,
              peer_wq, peer_k1, peer_k2, peer_u, peer_v, norm_final):
    b, l, _ = x.shape
    for i in range(DEPTH):
        hn = rmsnorm(x, norm_mix[i])
        proj = hn @ w_in[i]
        q, k, v, s5_u, ssd_z, ssd_xbc, ssd_dt, gates = _split_in_proj(proj)
        branch_a = sliding_window_attention(q, k, v, attn_sinks[i]) @ w_attn_out[i]
        ys5 = jax.nn.gelu(s5_mixer(s5_u, s5_lambda_re[i], s5_lambda_im[i], s5_log_dt[i], s5_b_re[i], s5_b_im[i],
                                   s5_c_re[i], s5_c_im[i], s5_d[i]))
        branch_b = (ys5 @ s5_glu_a[i]) * jax.nn.sigmoid(ys5 @ s5_glu_b[i])
        branch_c = ssd_mixer(ssd_z, ssd_xbc, ssd_dt, ssd_conv_w[i], ssd_conv_b[i], ssd_dt_bias[i], ssd_a_log[i],
                             ssd_d[i], ssd_norm[i]) @ w_ssd_out[i]
        g = jax.nn.sigmoid(gates.reshape(b, l, N_BRANCH, D_MODEL))
        merged = g[:, :, 0] * branch_a + g[:, :, 1] * branch_b + g[:, :, 2] * branch_c
        x = x + merged @ w_o[i]
        x = x + memory_cross_attention(rmsnorm(x, norm_xattn[i]), rmsnorm(mem, norm_mem[i]), xa_wq[i], xa_wkv[i], xa_wo[i])
        x = x + peer_ffn(rmsnorm(x, norm_ffn[i]), peer_wq[i], peer_k1[i], peer_k2[i], peer_u[i], peer_v[i])
    return rmsnorm(x, norm_final)


_drawn_inputs = setup_inputs


def setup_inputs(seed=0):
    import zlib

    import numpy as np

    out = dict(_drawn_inputs(seed))
    spreads = {}
    factors = {'s5_lambda_re': 8.0, 'norm_xattn': 4.161, 'norm_mem': 3.269, 'norm_final': 2.945}
    for name, (base, spread) in spreads.items():
        noise = np.random.default_rng([zlib.crc32(name.encode()), seed]).standard_normal(out[name].shape)
        drawn = base * np.exp(spread * noise) if base else spread * noise
        out[name] = __import__('jax').numpy.asarray(drawn.astype(out[name].dtype))
    for name, factor in factors.items():
        out[name] = (out[name] * factor).astype(out[name].dtype)
    return out
```

```python
from contextlib import ExitStack
import math

import numpy as np
import concourse.bass as bass
from concourse import mybir
from concourse.alu_op_type import AluOpType as ALU

F32, U32, I32 = mybir.dt.float32, mybir.dt.uint32, mybir.dt.int32
ACT = mybir.ActivationFunctionType
AX = mybir.AxisListType

P = 128
D = 1024
SEQ = 256
TT = SEQ // P
KT = D // P
HALF = 512
EPS = 1e-6
HEADS, KVH, REP, HD = 8, 2, 4, 64
S5W, S5TILES = 512, 16
SSDH = 16
XH = 4
PH, TOPK, NKEYS = 8, 16, 128
EXPERTS = NKEYS * NKEYS
MAGIC = 12582912.0
TWO_PI = 6.283185
NEG = -1e30

UNIT = 2048
RING = 4
U_QKVUX, U_Z, U_GATES, U_ATTN, U_XK, U_XV, U_GLU, U_SSD, U_WO, U_XQ, U_XO = 0, 10, 14, 26, 28, 29, 30, 34, 38, 42, 43
UNITS = 44
J_QKVUX, J_Z, J_GATES, J_ATTN, J_XK, J_XV, J_GLU, J_SSD, J_WO, J_XQ, J_XO = 0, 10, 14, 26, 30, 31, 32, 40, 44, 48, 49
JOBS = 53
JOBS_OF_UNIT = ([n + 1 for n in range(10)] + [12, 12, 14, 14] + [15 + n for n in range(12)] + [28, 30, 31, 32]
                + [36, 36, 40, 40] + [41, 42, 43, 44] + [46, 46, 48, 48] + [49, 53])

COLS = {}
_at = 0
for _name, _n in (("lr", 16), ("li", 16), ("ldt", 16), ("bre", 256), ("bim", 256), ("cre", 256), ("cim", 256),
                  ("s5d", 4), ("convw", 40), ("convb", 10), ("g_mix", 8), ("g_x", 8), ("g_mem", 8), ("g_ssd", 8),
                  ("dtb", 16), ("alog", 16), ("ssdd", 16), ("sinks", 8), ("wdt", 128), ("k1", 128), ("k2", 128)):
    COLS[_name] = (_at, _at + _n)
    _at += _n
NPAR = _at
CCOLS = {}
_at = 0
for _name, _n in (("ident", 128), ("later", 128), ("upto", 128), ("bias", 2048), ("time", 256), ("iota", 16)):
    CCOLS[_name] = (_at, _at + _n)
    _at += _n
NCONST = _at

SLOTS = 8
ROW = 2 * D


class Signal:

    def __init__(self, sem, per, pre=0):
        self.sem, self.per, self.pre = sem, per, pre

    def at(self, layer, k):
        return layer * self.per + (k + self.pre)


def build(nc, depth, x_d, mem_d, units_d, wq_d, par_d, const_d, gffn_d, gfin_d, table_d, out_d):
    ctx = ExitStack()
    with ctx:
        def sb(name, shape, dt=F32):
            return ctx.enter_context(nc.sbuf_tensor(name, shape, dt))

        def sig(name, per, pre=0):
            return Signal(ctx.enter_context(nc.semaphore(name)), per, pre)

        const = sb("const", [P, NCONST])
        par = sb("par", [P, NPAR])
        x = sb("x", [P, TT, D])
        xn = sb("xn", [P, TT, D])
        hT = sb("hT", [P, KT, SEQ])
        ring = sb("ring", [P, RING, UNIT])
        arena = sb("arena", [P, SLOTS * ROW])
        gates = sb("gates", [P, 24 * SEQ])
        memT = sb("memT", [P, KT, SEQ])
        zs = sb("zs", [P, TT, D])
        qT = sb("qT", [P, REP, SEQ])
        kT = sb("kT", [P, SEQ])
        vN = sb("vN", [P, TT, P])
        uT = sb("uT", [P, 4, SEQ])
        gnat = uT[:, :, :].rearrange("p a b -> p (a b)")
        xbcC = sb("xbcC", [P, 10, SEQ])
        kxT = sb("kxT", [P, 2, SEQ])
        vx = sb("vx", [P, TT, SEQ])
        small = sb("small", [P, 1024])

        def cst(name):
            return const[:, CCOLS[name][0]:CCOLS[name][1]]

        def pr(name):
            return par[:, COLS[name][0]:COLS[name][1]]

        def cut(t, start, *shape):
            n = int(np.prod(shape))
            v = t[:, start:start + n]
            if len(shape) == 2:
                v = v.rearrange("p (a b) -> p a b", b=shape[1])
            if len(shape) == 3:
                v = v.rearrange("p (a b c) -> p a b c", b=shape[1], c=shape[2])
            return v

        ident, later, upto = cst("ident"), cst("later"), cst("upto")
        bias = cst("bias").rearrange("p (h k) -> p h k", h=HEADS)

        sc0, sc1 = cut(gates, 0, HEADS, P), cut(gates, 1024, HEADS, 2 * P)
        pT0, pT1 = cut(gates, 3072, HEADS * P), cut(gates, 4096, TT, HEADS * P)
        gT = cut(gates, 0, 24, SEQ)
        Zr, Zi = cut(arena, 0, S5TILES, P), cut(arena, 2048, S5TILES, P)
        Cr, Ci = cut(arena, 4096, S5TILES, P), cut(arena, 6144, S5TILES, P)
        xbcT = cut(arena, 8192, 10, SEQ + 3)
        sn, cs = cut(arena, 8192, 2, HALF), cut(arena, 9216, 2, HALF)
        rot_r = cut(arena, 10240, HALF)
        phi = cut(arena, 10880, 2, HALF)
        rot_i, tmp1, tmp2, half_sin = (cut(arena, 11904 + HALF * i, HALF) for i in range(4))
        bb = cut(arena, 13440, 3, 256)
        hmT = cut(arena, 14336, KT, SEQ)
        xflat = xn[:, :, :].rearrange("p a b -> p (a b)")
        xr_, xi_ = cut(xflat, 0, 2, HALF), cut(xflat, 1024, 2, HALF)
        xsn, xdt = cut(arena, 0, TT, D), cut(arena, 2048, TT, D)
        adU, decayE = cut(arena, 4096, SSDH, P), cut(arena, 6144, SSDH, P)
        xdec, bN, s0 = cut(arena, 8192, D), cut(arena, 9216, P), cut(arena, 9344, HALF)
        cbm, ytmp = cut(arena, 9856, 4, P), cut(arena, 10368, D)
        sgate = cut(arena, 8192, 2, HALF)
        mergedT = cut(arena, 11392, KT, SEQ)
        memN = cut(arena, 0, TT, D)
        qxT, oxT = cut(arena, 0, 2, SEQ), cut(arena, 512, 2, SEQ)
        scx, pTx = cut(arena, 1024, TT, XH, SEQ), cut(arena, 3072, TT, XH, TT * P)
        wq = zs[:, :, :].rearrange("p a b -> p (a b)").rearrange("p (k c) -> p k c", k=KT)
        rows = arena[:, :].rearrange("p (s r) -> p s r", s=SLOTS)
        qh = cut(gates, 0, 2, SEQ)
        sk, skw = cut(gates, 512, 2 * TT, NKEYS), cut(gates, 1024, 2 * TT, NKEYS)
        cand, candw = cut(gates, 1536, TT, 256), cut(gates, 2048, TT, 256)
        onehot, picked = cut(gates, 2560, 2, 256), cut(gates, 3072, 2, 256)
        diag = cut(gates, 3584, 4, P)
        junk = cut(gates, 4096, D)

        _free = [0]

        def tiny(*shape):
            n = int(np.prod(shape))
            _free[0] += n
            assert _free[0] <= 1024
            return cut(small, _free[0] - n, *shape)

        ssq, ms, root, rstd = tiny(2), tiny(2), tiny(2), tiny(2)
        mx, nmx, sums, sinkd, esink = tiny(2, 8), tiny(2, 8), tiny(2, 8), tiny(2, 8), tiny(2, 8)
        dts5, la, th, mag, ar, ai, nr, den, wr, wi, t16a, t16b, th2pi = (tiny(16) for _ in range(13))
        ang, e_n, e_f, e_p, sn16, cs16 = (tiny(16) for _ in range(6))
        dts, ad, sp_a, sp_e, sp_l, sp_d = (tiny(TT, 16) for _ in range(6))
        nega, dec0, eac1 = tiny(16), tiny(16), tiny(16)
        mxx, sumx = tiny(2, 4), tiny(2, 4)
        act_dot, act_gelu, act_w = tiny(16), tiny(16), tiny(16)
        gcur, gnext = tiny(TT, 16), tiny(TT, 16)
        psum16 = tiny(2)
        layer_base = tiny(1)
        e_i = sb("e_i", [P, 16], I32)
        topv = sb("topv", [P, 2 * TT, 16])
        topi = sb("topi", [P, 2 * TT, 16], U32)
        topf = sb("topf", [P, 2 * TT, 16])
        ctop = sb("ctop", [P, TT, 16])
        cpos = sb("cpos", [P, TT, 16], U32)
        cab = sb("cab", [P, 2, 16], U32)
        cabf = sb("cabf", [P, 2, 16])
        eab = sb("eab", [P, 2, 16])
        eid = sb("eid", [P, 16])
        idx_next = sb("idx_next", [P, TT, 16], U32)
        idx = sb("idx", [P, TT, 16], U32)

        bank = [ctx.enter_context(nc.psum_tensor(f"bank{i}", [P, HALF], F32)) for i in range(8)]
        PJ, M = bank[0:2], bank[2:8]

        const_in = sig("const_in", 0, 0)
        x_in, mem_in = sig("x_in", 0), sig("mem_in", 0)
        par_in = sig("par_in", 16)
        gnat_in = sig("gnat_in", 16)
        unit_in = [sig(f"unit_in{r}", 16 * UNITS // RING) for r in range(RING)]
        wq_in = sig("wq_in", 16 * PH)
        row_in = [sig(f"row_in{s}", 16 * PH * TT * TOPK // SLOTS) for s in range(SLOTS)]
        out_done = sig("out_done", 0)
        ms_ready, root_ready = sig("ms_ready", 4, 1), sig("root_ready", 4, 1)
        xn_ready = sig("xn_ready", 8, 2)
        xT_full, hT_ready = sig("xT_full", 16, 4), sig("hT_ready", 16, 4)
        proj_full = sig("proj_full", JOBS)
        proj_free = [sig("proj_free0", 27), sig("proj_free1", 26)]
        score_full, score_read = sig("score_full", 4), sig("score_read", 1)
        max_ready, exp_ready, p_ready = sig("max_ready", 2), sig("exp_ready", 2), sig("p_ready", 2)
        pT_full, pT_ready = sig("pT_full", 6), sig("pT_ready", 6)
        o_full, oT_ready = sig("o_full", 2), sig("oT_ready", 2)
        s5_arg, s5_trig = sig("s5_arg", 1), sig("s5_trig", 1)
        bb_ready, frames_ready = sig("bb_ready", 1), sig("frames_ready", 1)
        zT_full, zT_ready = sig("zT_full", 8), sig("zT_ready", 8)
        phi_ready, frac_ready, trig_ready = sig("phi_ready", 8), sig("frac_ready", 8), sig("trig_ready", 8)
        bu_full, bu_read, state_ready, y_full = sig("bu_full", 8), sig("bu_read", 8), sig("state_ready", 8), sig("y_full", 8)
        ys5_pre, ys5_ready = sig("ys5_pre", 4), sig("ys5_ready", 4)
        conv_ready, silu_ready = sig("conv_ready", 2), sig("silu_ready", 2)
        dt_full, dt_arg, dt_exp, dt_one, dt_log, ad_ready = (sig(n, 1) for n in (
            "dt_full", "dt_arg", "dt_exp", "dt_one", "dt_log", "ad_ready"))
        xs_full, xs_ready = sig("xs_full", 4), sig("xs_ready", 4)
        misc_full, misc_ready = sig("misc_full", 1), sig("misc_ready", 1)
        cb_full, cb_ready = sig("cb_full", 1), sig("cb_ready", 1)
        adU_ready, diff_full, decay_ready = sig("adU_ready", 2), sig("diff_full", 8), sig("decay_ready", 8)
        w_ready, xdec_ready, yd_full, yd_read = sig("w_ready", 2), sig("xdec_ready", 1), sig("yd_full", 2), sig("yd_read", 2)
        s0_full, s0_ready, yo_full = sig("s0_full", 1), sig("s0_ready", 1), sig("yo_full", 1)
        hmT_ready = sig("hmT_ready", 1)
        sg_ready, sg_used = sig("sg_ready", 4), sig("sg_used", 4)
        merged_ready = sig("merged_ready", 1)
        sx_full, mxx_ready, expx_ready, px_ready = sig("sx_full", 2), sig("mxx_ready", 2), sig("expx_ready", 2), sig("px_ready", 2)
        pTx_full, pTx_ready, ox_full, ox_ready = sig("pTx_full", 4), sig("pTx_ready", 4), sig("ox_full", 2), sig("ox_ready", 2)
        hn_ready = sig("hn_ready", 1)
        qh_full, qh_ready = sig("qh_full", PH), sig("qh_ready", PH)
        sk_full, sk_ready = sig("sk_full", PH), sig("sk_ready", PH)
        top_ready, topexp_ready = sig("top_ready", PH * TT), sig("topexp_ready", PH * TT)
        idx_ready = sig("idx_ready", PH * TT)
        dot_ready = sig("dot_ready", PH * TT * TOPK)
        diag_ready = sig("diag_ready", PH * TT * TOPK)
        row_used = sig("row_used", PH * TT * TOPK)
        peer_added = sig("peer_added", PH * TT)
        gather_go = sig("gather_go", 0)
        routed = sig("routed", PH)

        block = ctx.enter_context(nc.Block())

        @block.sync
        def _(sp):
            sp.dma_start(const[:, :], const_d).then_inc(const_in.sem, 16)
            sp.dma_start(arena[:, 0:TT * D].rearrange("p (t d) -> p t d", t=TT),
                         mem_d.rearrange("b (t p) d -> p (b t) d", p=P)).then_inc(mem_in.sem, 16)
            sp.dma_start(x[:, :, :], x_d.rearrange("b (t p) d -> p (b t) d", p=P)).then_inc(x_in.sem, 16)
            sp.dma_start(par[:, :], par_d[0]).then_inc(par_in.sem, 16)
            for n in range(RING):
                sp.dma_start(ring[:, n, :], units_d[n]).then_inc(unit_in[n].sem, 16)
            with sp.Fori(0, depth) as L:
                for n in range(UNITS):
                    sp.wait_ge(proj_full.sem, proj_full.at(L, JOBS_OF_UNIT[n]))
                    sp.dma_start(ring[:, n % RING, :], units_d[L * UNITS + (n + RING)]).then_inc(
                        unit_in[n % RING].sem, 16)
                    if n == U_SSD:
                        sp.wait_ge(xn_ready.sem, xn_ready.at(L, 4))
                        sp.dma_start(gnat, gffn_d[L].partition_broadcast(P)).then_inc(gnat_in.sem, 16)
                        sp.dma_start(wq[:, :, :], wq_d[L * PH].rearrange("p (k c) -> p k c", k=KT)).then_inc(
                            wq_in.sem, 16)
                with sp.Fori(1, PH) as h:
                    sp.wait_ge(qh_full.sem, qh_full.at(L, h))
                    sp.dma_start(wq[:, :, :], wq_d[L * PH + h].rearrange("p (k c) -> p k c", k=KT)).then_inc(
                        wq_in.sem, 16)
                sp.wait_ge(sk_full.sem, sk_full.at(L, PH))
                sp.dma_start(par[:, :], par_d[L + 1]).then_inc(par_in.sem, 16)
            sp.wait_ge(hn_ready.sem, depth)
            sp.dma_start(gnat, gfin_d.partition_broadcast(P)).then_inc(gnat_in.sem, 16)
            sp.wait_ge(xn_ready.sem, xn_ready.at(depth, 2))
            sp.dma_start(out_d.rearrange("b (t p) d -> p (b t) d", p=P), xn[:, :, :]).then_inc(out_done.sem, 16)
            sp.wait_ge(out_done.sem, 16)
            for n in range(RING):
                sp.wait_ge(unit_in[n].sem, unit_in[n].per * depth + 16)
            sp.wait_ge(par_in.sem, 16 * (depth + 1))

        @block.gpsimd
        def _(pool):

            def gathers(L, h, first):
                for tt in range(TT):
                    pool.wait_ge(idx_ready.sem, idx_ready.at(L, h * TT + (tt + 1)))
                    nc.gpsimd.sem_inc(gather_go.sem, 1)
                    for k in range(TOPK):
                        if not (first and tt == 0 and k < SLOTS):
                            pool.wait_ge(row_used.sem, row_used.at(L, h * (TT * TOPK) + (tt * TOPK + k + 1 - SLOTS)))
                            nc.gpsimd.sem_inc(gather_go.sem, 1)
                        pool.indirect_dma_start(
                            out=rows[:, k % SLOTS, :], out_offset=None, in_=table_d,
                            in_offset=bass.IndirectOffsetOnAxis(ap=idx[:, tt, k:k + 1], axis=0),
                        ).then_inc(row_in[k % SLOTS].sem, 16)

            def into_frames(dst, src, scale):
                for b in range(4):
                    for g in range(2):
                        o = cut4(dst)[64 * g:64 * g + 64, :, b, 32 * b + 16 * g:32 * b + 16 * g + 16]
                        i = src.rearrange("p (a b i) -> p a b i", b=4, i=16)[64 * g:64 * g + 64, :, b, :]
                        last = nc.gpsimd.tensor_scalar(o, i, scale, 0.0, ALU.mult, ALU.add)
                return last

            def cut4(t):
                return t.rearrange("p (a b) c -> p a b c", b=4)

            with pool.Fori(0, depth) as L:
                pool.wait_ge(par_in.sem, par_in.at(L, 16))
                pool.wait_ge(hT_ready.sem, hT_ready.at(L, 4))
                nc.gpsimd.sem_inc(gather_go.sem, 1)
                nc.gpsimd.memset(arena[:, 0:8192], 0.0)
                pool.drain()
                into_frames(Cr, pr("cre"), 1.0)
                into_frames(Ci, pr("cim"), -1.0)
                pool.wait_ge(bb_ready.sem, bb_ready.at(L, 1))
                nc.gpsimd.sem_inc(gather_go.sem, 1)
                into_frames(Zr, bb[:, 0, :], 1.0)
                into_frames(Zi, bb[:, 1, :], 1.0).then_inc(frames_ready.sem, 1)
                pool.drain()
                nc.gpsimd.tensor_tensor(hmT, memT[:, :, :], pr("g_mem").unsqueeze(2).to_broadcast([P, KT, SEQ]),
                                        ALU.mult).then_inc(hmT_ready.sem, 1)
                for s in range(8):
                    if s >= 2:
                        pool.wait_ge(trig_ready.sem, trig_ready.at(L, s - 1))
                    nc.gpsimd.tensor_tensor(
                        phi[:, s % 2, :].rearrange("p (a t) -> p a t", a=2),
                        th2pi[:, 2 * s:2 * s + 2].unsqueeze(2).to_broadcast([P, 2, SEQ]),
                        cst("time").unsqueeze(1).to_broadcast([P, 2, SEQ]), ALU.mult).then_inc(phi_ready.sem, 1)
                gathers(L, 0, True)
                with pool.Fori(1, PH) as h:
                    gathers(L, h, False)

        @block.tensor
        def _(pe):

            def transposes(xn_at, full):
                for tt in range(TT):
                    pe.wait_ge(xn_ready.sem, xn_at(tt + 1))
                    for half in range(2):
                        for i in range(4):
                            c = (4 * half + i) * P
                            t = nc.tensor.transpose(M[2 * tt + half][:, i * P:(i + 1) * P], xn[:, tt, c:c + P], ident)
                        t.then_inc(full.sem, 1)

            pe.wait_ge(const_in.sem, 16)
            transposes(lambda k: k, xT_full)

            def peer_scores(L, h):
                pe.wait_ge(wq_in.sem, wq_in.at(L, h * 16 + 16))
                for half in range(2):
                    for kt in range(KT):
                        m = nc.tensor.matmul(PJ[0][:, half * SEQ:(half + 1) * SEQ], wq[:, kt, half * P:(half + 1) * P],
                                             hT[:, kt, :], start=(kt == 0), stop=(kt == KT - 1))
                m.then_inc(qh_full.sem, 1)
                pe.wait_ge(qh_ready.sem, qh_ready.at(L, h + 1))
                for tt in range(TT):
                    for half in range(2):
                        r = 2 * tt + half
                        m = nc.tensor.matmul(PJ[1][:, r * NKEYS:(r + 1) * NKEYS], qh[:, half, tt * P:(tt + 1) * P],
                                             pr(("k1", "k2")[half]), start=True, stop=True)
                m.then_inc(sk_full.sem, 1)

            def peer_mix(L, h):
                for tt in range(TT):
                    for k in range(TOPK):
                        n = tt * TOPK + k
                        if k == 0:
                            pass
                        pe.wait_ge(diag_ready.sem, diag_ready.at(L, h * (TT * TOPK) + (n + 1)))
                        for half in range(2):
                            m = nc.tensor.matmul(M[2 * tt + half][:, :], diag[:, k % 4, :],
                                                 rows[:, k % SLOTS, D + half * HALF:D + (half + 1) * HALF],
                                                 start=(k == 0), stop=(k == TOPK - 1))
                        m.then_inc(row_used.sem, 1)

            with pe.Fori(0, depth) as L:
                def unit(n):
                    pe.wait_ge(unit_in[n % RING].sem, unit_in[n % RING].at(L, 16 * (n // RING + 1)))
                    return ring[:, n % RING, :]

                def job(j):
                    if j >= 2:
                        pe.wait_ge(proj_free[j % 2].sem, proj_free[j % 2].at(L, j // 2))
                    return PJ[j % 2]

                def columns_T(j, w, tiles, src, kts):
                    out = job(j)
                    for i, c in enumerate(tiles):
                        for kt in range(kts):
                            m = nc.tensor.matmul(out[:, i * SEQ:(i + 1) * SEQ], w[:, c, kt, :], src[:, kt, :],
                                                 start=(kt == 0), stop=(kt == kts - 1))
                    m.then_inc(proj_full.sem, 1)

                def rows_N(j, u, src):
                    for kh in range(2):
                        w = unit(u + kh).rearrange("p (k c) -> p k c", k=4)
                        for tt in range(TT):
                            out = job(j + tt) if kh == 0 else PJ[(j + tt) % 2]
                            for k in range(4):
                                m = nc.tensor.matmul(out[:, :], src[:, 4 * kh + k, tt * P:(tt + 1) * P], w[:, k, :],
                                                     start=(kh == 0 and k == 0), stop=(kh == 1 and k == 3))
                            if kh == 1:
                                m.then_inc(proj_full.sem, 1)

                def pair(n, **kw):
                    return unit(n).rearrange("p (i k c) -> p i k c", i=2, k=KT)

                transposes(lambda k: xn_ready.at(L, k), xT_full)
                pe.wait_ge(hT_ready.sem, hT_ready.at(L, 4))
                pe.wait_ge(par_in.sem, par_in.at(L, 16))

                def qkvux(n):
                    w = pair(U_QKVUX + n)
                    if n != 2:
                        return columns_T(J_QKVUX + n, w, (0, 1), hT, KT)
                    out = job(J_QKVUX + n)
                    for kt in range(KT):
                        nc.tensor.matmul(out[:, 0:SEQ], w[:, 0, kt, :], hT[:, kt, :], start=(kt == 0), stop=(kt == KT - 1))
                    for tt in range(TT):
                        for kt in range(KT):
                            m = nc.tensor.matmul(out[:, SEQ + tt * P:SEQ + (tt + 1) * P], hT[:, kt, tt * P:(tt + 1) * P],
                                                 w[:, 1, kt, :], start=(kt == 0), stop=(kt == KT - 1))
                    m.then_inc(proj_full.sem, 1)

                for n in range(3):
                    qkvux(n)
                pe.wait_ge(proj_free[0].sem, proj_free[0].at(L, 2))
                pe.wait_ge(proj_free[1].sem, proj_free[1].at(L, 1))
                for G in range(KVH):
                    g = slice(64 * G, 64 * G + 64)
                    for j in range(REP):
                        m = nc.tensor.matmul(M[G][:, j * P:(j + 1) * P], qT[g, j, 0:P], kT[g, 0:P], start=True, stop=True)
                    m.then_inc(score_full.sem, 1)
                for G in range(KVH):
                    g = slice(64 * G, 64 * G + 64)
                    for j in range(REP):
                        m = nc.tensor.matmul(M[2 + 2 * G + j // 2][:, (j % 2) * SEQ:(j % 2 + 1) * SEQ], qT[g, j, P:SEQ],
                                             kT[g, :], start=True, stop=True)
                    m.then_inc(score_full.sem, 1)
                for n in range(3, 10):
                    qkvux(n)
                pe.wait_ge(score_read.sem, score_read.at(L, 1))
                wdt = pr("wdt").rearrange("p (k c) -> p k c", k=KT)
                for tt in range(TT):
                    for kt in range(KT):
                        m = nc.tensor.matmul(M[5][:, tt * 16:(tt + 1) * 16], hT[:, kt, tt * P:(tt + 1) * P], wdt[:, kt, :],
                                             start=(kt == 0), stop=(kt == KT - 1))
                m.then_inc(dt_full.sem, 1)
                pe.wait_ge(p_ready.sem, p_ready.at(L, 1))
                for G in range(KVH):
                    for j in range(REP):
                        t = nc.tensor.transpose(M[2 + G][:, j * P:(j + 1) * P], sc0[:, 4 * G + j, :], ident)
                    t.then_inc(pT_full.sem, 1)
                pe.wait_ge(pT_ready.sem, pT_ready.at(L, 2))
                for G in range(KVH):
                    m = nc.tensor.matmul(M[4][64 * G:64 * G + 64, :], vN[:, 0, 64 * G:64 * G + 64],
                                         pT0[:, G * HALF:(G + 1) * HALF], start=True, stop=True)
                m.then_inc(o_full.sem, 1)
                rows_N(J_Z, U_Z, hT)
                pe.wait_ge(p_ready.sem, p_ready.at(L, 2))
                for kb in range(TT):
                    for G in range(KVH):
                        for j in range(REP):
                            t = nc.tensor.transpose(M[2 * kb + G][:, j * P:(j + 1) * P],
                                                    sc1[:, 4 * G + j, kb * P:(kb + 1) * P], ident)
                        t.then_inc(pT_full.sem, 1)
                pe.wait_ge(pT_ready.sem, pT_ready.at(L, 6))
                pe.wait_ge(oT_ready.sem, oT_ready.at(L, 1))
                for G in range(KVH):
                    for kb in range(TT):
                        m = nc.tensor.matmul(M[4][64 * G:64 * G + 64, :], vN[:, kb, 64 * G:64 * G + 64],
                                             pT1[:, kb, G * HALF:(G + 1) * HALF], start=(kb == 0), stop=(kb == 1))
                m.then_inc(o_full.sem, 1)
                rows_N(J_Z + 2, U_Z + 2, hT)
                pe.wait_ge(frames_ready.sem, frames_ready.at(L, 1))
                for q in range(8):
                    Z = (Zr, Zi)[q // 4]
                    if q >= 4:
                        pe.wait_ge(zT_ready.sem, zT_ready.at(L, q - 3))
                    for i in range(4):
                        t = nc.tensor.transpose(M[q % 4][:, i * P:(i + 1) * P], Z[:, 4 * (q % 4) + i, :], ident)
                    t.then_inc(zT_full.sem, 1)
                pe.wait_ge(zT_ready.sem, zT_ready.at(L, 8))

                def s5_outputs(s):
                    c = s // 2
                    pe.wait_ge(state_ready.sem, state_ready.at(L, s + 1))
                    if s == 0:
                        pe.wait_ge(oT_ready.sem, oT_ready.at(L, 2))
                    if s == 2:
                        pe.wait_ge(dt_arg.sem, dt_arg.at(L, 1))
                    if s % 2 == 0 and c >= 2:
                        pe.wait_ge(ys5_pre.sem, ys5_pre.at(L, c - 1))
                    for i in range(2):
                        for part, (mat, val) in enumerate(((Cr, xr_), (Ci, xi_))):
                            m = nc.tensor.matmul(M[4 + c % 2][:, 0:SEQ], mat[:, 2 * s + i, :],
                                                 val[:, s % 2, i * SEQ:(i + 1) * SEQ],
                                                 start=(s % 2 == 0 and i == 0 and part == 0),
                                                 stop=(s % 2 == 1 and i == 1 and part == 1))
                    m.then_inc(y_full.sem, 1)

                for s in range(8):
                    if s >= 2:
                        pe.wait_ge(bu_read.sem, bu_read.at(L, s - 1))
                    for part, Z in enumerate((Zr, Zi)):
                        for i in range(2):
                            m = nc.tensor.matmul(M[2 * (s % 2) + part][:, i * SEQ:(i + 1) * SEQ], Z[:, 2 * s + i, :],
                                                 uT[:, s // 2, :], start=True, stop=True)
                    m.then_inc(bu_full.sem, 1)
                    columns_T(J_GATES + s, pair(U_GATES + s), (0, 1), hT, KT)
                    if s >= 1:
                        s5_outputs(s - 1)
                s5_outputs(7)
                pe.wait_ge(silu_ready.sem, silu_ready.at(L, 2))
                for c in range(2):
                    for half in range(2):
                        for i in range(4):
                            t = nc.tensor.transpose(M[2 * c + half][:, i * P:(i + 1) * P],
                                                    xbcC[:, 4 * half + i, c * P:(c + 1) * P], ident)
                        t.then_inc(xs_full.sem, 1)
                columns_T(J_GATES + 8, pair(U_GATES + 8), (0, 1), hT, KT)
                pe.wait_ge(ys5_pre.sem, ys5_pre.at(L, 4))
                pe.wait_ge(ad_ready.sem, ad_ready.at(L, 1))
                nc.tensor.transpose(M[4][:, 0:P], xbcC[:, 8, 0:P], ident)
                nc.tensor.matmul(M[4][:, 256:272], later, ad[:, 0, :], start=True, stop=True)
                nc.tensor.matmul(M[4][:, 272:288], upto, ad[:, 1, :], start=True, stop=True).then_inc(misc_full.sem, 1)
                for g in range(2):
                    pe.drain()
                    for c in range(2):
                        r = slice(64 * g, 64 * g + 64)
                        q = 2 * c + g
                        m = nc.tensor.matmul(M[5][:, q * P:(q + 1) * P], xbcC[r, 8, c * P:(c + 1) * P],
                                             xbcC[r, 9, c * P:(c + 1) * P], start=True, stop=True)
                m.then_inc(cb_full.sem, 1)
                columns_T(J_GATES + 9, pair(U_GATES + 9), (0, 1), hT, KT)

                def ssd_decays(c):
                    pe.wait_ge(adU_ready.sem, adU_ready.at(L, c + 1))
                    if c == 0:
                        pe.wait_ge(xs_ready.sem, xs_ready.at(L, 4))
                    else:
                        pe.wait_ge(s0_ready.sem, s0_ready.at(L, 1))
                    for q in range(4):
                        nc.tensor.matmul(M[q][:, :], later, adU[:, 4 * q:4 * q + 4, :], start=True, stop=True).then_inc(
                            diff_full.sem, 1)

                def ssd_diagonal(c):
                    pe.wait_ge(w_ready.sem, w_ready.at(L, c + 1))
                    if c == 0:
                        pe.wait_ge(misc_ready.sem, misc_ready.at(L, 1))
                    else:
                        pe.wait_ge(yd_read.sem, yd_read.at(L, 1))
                    for h in range(SSDH):
                        m = nc.tensor.matmul(M[4 + h // 8][:, (h % 8) * HD:(h % 8 + 1) * HD], decayE[:, h, :],
                                             xdt[:, c, h * HD:(h + 1) * HD], start=True, stop=True)
                    m.then_inc(yd_full.sem, 1)

                ssd_decays(0)
                columns_T(J_GATES + 10, pair(U_GATES + 10), (0, 1), hT, KT)
                ssd_diagonal(0)
                pe.wait_ge(xdec_ready.sem, xdec_ready.at(L, 1))
                for g in range(2):
                    m = nc.tensor.matmul(M[0][64 * g:64 * g + 64, :], bN[:, 64 * g:64 * g + 64],
                                         xdec[:, g * HALF:(g + 1) * HALF], start=True, stop=True)
                m.then_inc(s0_full.sem, 1)
                columns_T(J_GATES + 11, pair(U_GATES + 11), (0, 1), hT, KT)
                ssd_decays(1)
                attn_units = [unit(U_ATTN + i).rearrange("p (i k c) -> p i k c", i=4, k=4) for i in range(1)]
                for i in range(4):
                    if i == 2:
                        attn_units.append(unit(U_ATTN + 1).rearrange("p (i k c) -> p i k c", i=4, k=4))
                    columns_T(J_ATTN + i, attn_units[i // 2], (2 * (i % 2), 2 * (i % 2) + 1), qT, 4)
                pe.wait_ge(hmT_ready.sem, hmT_ready.at(L, 1))
                columns_T(J_XK, pair(U_XK), (0, 1), hmT, KT)
                out = job(J_XV)
                w = unit(U_XV).rearrange("p (k c) -> p k c", k=KT)
                for tt in range(TT):
                    for kt in range(KT):
                        m = nc.tensor.matmul(out[:, tt * SEQ:(tt + 1) * SEQ], hmT[:, kt, tt * P:(tt + 1) * P], w[:, kt, :],
                                             start=(kt == 0), stop=(kt == KT - 1))
                m.then_inc(proj_full.sem, 1)
                ssd_diagonal(1)
                pe.wait_ge(decay_ready.sem, decay_ready.at(L, 8))
                for g in range(2):
                    m = nc.tensor.matmul(M[g][:, :], xbcC[64 * g:64 * g + 64, 9, P:SEQ], s0[64 * g:64 * g + 64, :],
                                         start=True, stop=True)
                m.then_inc(yo_full.sem, 1)
                pe.wait_ge(ys5_ready.sem, ys5_ready.at(L, 4))
                for i in range(4):
                    if i % 2 == 0:
                        wa = unit(U_GLU + i).rearrange("p (i k c) -> p i k c", i=4, k=4)
                        wb = unit(U_GLU + i + 1).rearrange("p (i k c) -> p i k c", i=4, k=4)
                    cols = (2 * (i % 2), 2 * (i % 2) + 1)
                    columns_T(J_GLU + 2 * i, wa, cols, uT, 4)
                    columns_T(J_GLU + 2 * i + 1, wb, cols, uT, 4)
                transposes(lambda k: xn_ready.at(L, 2 + k), xT_full)
                pe.wait_ge(hT_ready.sem, hT_ready.at(L, 8))
                for i in range(4):
                    columns_T(J_SSD + i, pair(U_SSD + i), (0, 1), hT, KT)
                pe.wait_ge(merged_ready.sem, merged_ready.at(L, 1))
                rows_N(J_WO, U_WO, mergedT)
                rows_N(J_WO + 2, U_WO + 2, mergedT)
                transposes(lambda k: xn_ready.at(L, 4 + k), xT_full)
                pe.wait_ge(hT_ready.sem, hT_ready.at(L, 12))
                columns_T(J_XQ, pair(U_XQ), (0, 1), hT, KT)
                pe.wait_ge(proj_free[0].sem, proj_free[0].at(L, J_XQ // 2 + 1))
                for tt in range(TT):
                    for h in range(XH):
                        r = slice(64 * (h % 2), 64 * (h % 2) + 64)
                        m = nc.tensor.matmul(M[2 * tt + h % 2][:, (h // 2) * SEQ:(h // 2 + 1) * SEQ],
                                             qxT[r, h // 2, tt * P:(tt + 1) * P], kxT[r, h // 2, :], start=True, stop=True)
                    m.then_inc(sx_full.sem, 1)
                for tt in range(TT):
                    pe.wait_ge(px_ready.sem, px_ready.at(L, tt + 1))
                    for kb in range(TT):
                        for h in range(XH):
                            t = nc.tensor.transpose(M[(4, 0)[tt] + kb][:, h * P:(h + 1) * P],
                                                    scx[:, tt, h, kb * P:(kb + 1) * P], ident)
                        t.then_inc(pTx_full.sem, 1)
                pe.wait_ge(px_ready.sem, px_ready.at(L, 2))
                def at_bank(h):
                    return 2 * (h % 2) + h // 2

                for tt in range(TT):
                    pe.wait_ge(pTx_ready.sem, pTx_ready.at(L, 2 * tt + 2))
                    for h in range(XH):
                        for kb in range(TT):
                            m = nc.tensor.matmul(
                                M[2 + tt][64 * (h % 2):64 * (h % 2) + 64, (h // 2) * P:(h // 2 + 1) * P],
                                vx[:, kb, h * HD:(h + 1) * HD], pTx[:, tt, :, :].rearrange("p h k -> p (h k)")[
                                    :, kb * HALF + at_bank(h) * P:kb * HALF + (at_bank(h) + 1) * P], start=(kb == 0), stop=(kb == 1))
                    m.then_inc(ox_full.sem, 1)
                pe.wait_ge(ox_ready.sem, ox_ready.at(L, 2))
                w = unit(U_XO).rearrange("p (k c) -> p k c", k=2)
                for tt in range(TT):
                    for c in range(2):
                        out = job(J_XO + 2 * tt + c)
                        for k in range(2):
                            m = nc.tensor.matmul(out[:, :], oxT[:, k, tt * P:(tt + 1) * P],
                                                 w[:, k, c * HALF:(c + 1) * HALF], start=(k == 0), stop=(k == 1))
                        m.then_inc(proj_full.sem, 1)
                transposes(lambda k: xn_ready.at(L, 6 + k), xT_full)
                pe.wait_ge(hT_ready.sem, hT_ready.at(L, 16))
                peer_scores(L, 0)
                with pe.Fori(0, PH - 1) as h:
                    peer_scores(L, h + 1)
                    peer_mix(L, h)
                peer_mix(L, PH - 1)

        @block.scalar
        def _(act):
            A = nc.scalar.activation

            def norm_root(need, done):
                act.wait_ge(ms_ready.sem, need)
                A(root, ms, ACT.Sqrt).then_inc(root_ready.sem, 1)

            norm_root(1, 1)

            def sin_cos(frac, s, c, hs):
                A(s, frac, ACT.Sin, scale=TWO_PI)
                A(hs, frac, ACT.Sin, scale=TWO_PI / 2)
                act.drain()
                A(hs, hs, ACT.Square)
                act.drain()
                return A(c, hs, ACT.Copy, scale=-2.0, bias=1.0)

            with act.Fori(0, depth) as L:
                def evac(j, out, func=ACT.Copy, **kw):
                    act.wait_ge(proj_full.sem, proj_full.at(L, j + 1))
                    n = out.shape
                    src = PJ[j % 2][:, :] if len(n) == 2 else PJ[j % 2][:, :].rearrange("p (a b) -> p a b", a=n[1])
                    A(out, src, func, **kw).then_inc(proj_free[j % 2].sem, 1)

                norm_root(ms_ready.at(L, 1), 1)
                act.wait_ge(s5_arg.sem, s5_arg.at(L, 1))
                sin_cos(ang, sn16, cs16, e_p).then_inc(s5_trig.sem, 1)
                evac(0, qT[:, 0:2, :])
                evac(1, qT[:, 2:4, :])
                act.wait_ge(proj_full.sem, proj_full.at(L, 3))
                A(kT[:, :], PJ[0][:, 0:SEQ], ACT.Copy)
                A(vN[:, :, :], PJ[0][:, SEQ:2 * SEQ].rearrange("p (a b) -> p a b", a=TT), ACT.Copy).then_inc(
                    proj_free[0].sem, 1)
                evac(3, uT[:, 0:2, :])
                evac(4, uT[:, 2:4, :])
                for n in range(5):
                    evac(5 + n, xbcT[:, 2 * n:2 * n + 2, 3:3 + SEQ])
                for tt in range(TT):
                    act.wait_ge(max_ready.sem, max_ready.at(L, tt + 1))
                    s = (sc0, sc1)[tt]
                    for h in range(HEADS):
                        A(s[:, h, :], s[:, h, :], ACT.Exp, bias=nmx[:, tt, h:h + 1], accum_out=sums[:, tt, h:h + 1])
                    A(esink[:, tt, :], sinkd[:, tt, :], ACT.Exp).then_inc(exp_ready.sem, 1)
                act.wait_ge(dt_arg.sem, dt_arg.at(L, 1))
                A(sp_e, sp_a, ACT.Exp, scale=-1.0)
                A(nega, pr("alog"), ACT.Exp).then_inc(dt_exp.sem, 1)
                act.wait_ge(dt_one.sem, dt_one.at(L, 1))
                A(sp_l, sp_d, ACT.Ln).then_inc(dt_log.sem, 1)
                for G in range(2):
                    act.wait_ge(pT_full.sem, pT_full.at(L, G + 1))
                    A(pT0[:, G * HALF:(G + 1) * HALF], M[2 + G][:, :], ACT.Copy).then_inc(pT_ready.sem, 1)
                act.wait_ge(o_full.sem, o_full.at(L, 1))
                A(qT[:, :, 0:P], M[4][:, :].rearrange("p (j t) -> p j t", j=REP), ACT.Copy).then_inc(oT_ready.sem, 1)
                evac(J_Z, zs[:, 0, 0:HALF], ACT.Silu)
                evac(J_Z + 1, zs[:, 1, 0:HALF], ACT.Silu)
                for q in range(4):
                    act.wait_ge(pT_full.sem, pT_full.at(L, 3 + q))
                    A(pT1[:, q // 2, (q % 2) * HALF:(q % 2 + 1) * HALF], M[q][:, :], ACT.Copy).then_inc(pT_ready.sem, 1)
                act.wait_ge(o_full.sem, o_full.at(L, 2))
                A(qT[:, :, P:SEQ], M[4][:, :].rearrange("p (j t) -> p j t", j=REP), ACT.Copy).then_inc(oT_ready.sem, 1)
                evac(J_Z + 2, zs[:, 0, HALF:D], ACT.Silu)
                evac(J_Z + 3, zs[:, 1, HALF:D], ACT.Silu)
                for half in range(2):
                    act.wait_ge(conv_ready.sem, conv_ready.at(L, half + 1))
                    A(xbcC[:, 5 * half:5 * half + 5, :], xbcC[:, 5 * half:5 * half + 5, :], ACT.Silu).then_inc(
                        silu_ready.sem, 1)
                for q in range(8):
                    act.wait_ge(zT_full.sem, zT_full.at(L, q + 1))
                    A((Zr, Zi)[q // 4][:, 4 * (q % 4):4 * (q % 4) + 4, :],
                      M[q % 4][:, :].rearrange("p (i c) -> p i c", i=4), ACT.Copy).then_inc(zT_ready.sem, 1)

                def turns(s):
                    act.drain()
                    act.wait_ge(frac_ready.sem, frac_ready.at(L, s + 1))
                    if s >= 2:
                        act.wait_ge(state_ready.sem, state_ready.at(L, s - 1))
                    sin_cos(phi[:, s % 2, :], sn[:, s % 2, :], cs[:, s % 2, :], half_sin).then_inc(trig_ready.sem, 1)

                def s5_gelu(c):
                    act.wait_ge(ys5_pre.sem, ys5_pre.at(L, c + 1))
                    A(uT[:, c, :], uT[:, c, :], ACT.Gelu_apprx_tanh).then_inc(ys5_ready.sem, 1)

                turns(0)
                for s in range(8):
                    if s < 7:
                        turns(s + 1)
                    evac(J_GATES + s, gT[:, 2 * s:2 * s + 2, :], ACT.Sigmoid)
                for c in range(4):
                    s5_gelu(c)
                for c in range(2):
                    for half in range(2):
                        act.wait_ge(xs_full.sem, xs_full.at(L, 2 * c + half + 1))
                        A(xsn[:, c, half * HALF:(half + 1) * HALF], M[2 * c + half][:, :], ACT.Copy).then_inc(xs_ready.sem, 1)
                evac(J_GATES + 8, gT[:, 16:18, :], ACT.Sigmoid)
                act.wait_ge(misc_full.sem, misc_full.at(L, 1))
                A(bN, M[4][:, 0:P], ACT.Copy)
                A(dec0, M[4][:, 256:272], ACT.Exp)
                A(eac1, M[4][:, 272:288], ACT.Exp).then_inc(misc_ready.sem, 1)
                evac(J_GATES + 9, gT[:, 18:20, :], ACT.Sigmoid)

                def decays(c):
                    for q in range(4):
                        act.wait_ge(diff_full.sem, diff_full.at(L, 4 * c + q + 1))
                        if c == 1 and q == 0:
                            act.wait_ge(yd_full.sem, yd_full.at(L, 1))
                        A(decayE[:, 4 * q:4 * q + 4, :], M[q][:, :].rearrange("p (h l) -> p h l", h=4),
                          ACT.Exp).then_inc(decay_ready.sem, 1)

                decays(0)
                evac(J_GATES + 10, gT[:, 20:22, :], ACT.Sigmoid)
                act.wait_ge(s0_full.sem, s0_full.at(L, 1))
                A(s0, M[0][:, :], ACT.Copy).then_inc(s0_ready.sem, 1)
                evac(J_GATES + 11, gT[:, 22:24, :], ACT.Sigmoid)
                decays(1)
                evac(J_XK, kxT[:, :, :])
                evac(J_XV, vx[:, :, :])
                for i in range(4):
                    if i >= 2:
                        act.wait_ge(sg_used.sem, sg_used.at(L, i - 1))
                    evac(J_GLU + 2 * i + 1, sgate[:, i % 2, :], ACT.Sigmoid)
                    act.drain()
                    A(small[:, 1023:1024], small[:, 1023:1024], ACT.Copy).then_inc(sg_ready.sem, 1)
                norm_root(ms_ready.at(L, 2), 1)
                norm_root(ms_ready.at(L, 3), 1)
                evac(J_XQ, qxT)
                for tt in range(TT):
                    act.wait_ge(mxx_ready.sem, mxx_ready.at(L, tt + 1))
                    for h in range(XH):
                        A(scx[:, tt, h, :], M[2 * tt + h // 2][:, (h % 2) * SEQ:(h % 2 + 1) * SEQ], ACT.Exp,
                          scale=HD ** -0.5, bias=mxx[:, tt, h:h + 1], accum_out=sumx[:, tt, h:h + 1])
                    A(small[:, 1023:1024], small[:, 1023:1024], ACT.Copy).then_inc(expx_ready.sem, 1)
                    act.drain()
                for tt in range(TT):
                    for kb in range(TT):
                        act.wait_ge(pTx_full.sem, pTx_full.at(L, 2 * tt + kb + 1))
                        A(pTx[:, tt, :, :].rearrange("p h k -> p (h k)")[:, kb * HALF:(kb + 1) * HALF],
                          M[(4, 0)[tt] + kb][:, :], ACT.Copy).then_inc(pTx_ready.sem, 1)
                for tt in range(TT):
                    act.wait_ge(ox_full.sem, ox_full.at(L, tt + 1))
                    A(oxT[:, :, tt * P:(tt + 1) * P], M[2 + tt][:, 0:2 * P].rearrange("p (j t) -> p j t", j=2),
                      ACT.Copy).then_inc(ox_ready.sem, 1)
                norm_root(ms_ready.at(L, 4), 1)

                def peer_out(h):
                    act.wait_ge(qh_full.sem, qh_full.at(L, h + 1))
                    A(qh, PJ[0][:, :].rearrange("p (a t) -> p a t", a=2), ACT.Copy).then_inc(qh_ready.sem, 1)
                    act.wait_ge(sk_full.sem, sk_full.at(L, h + 1))
                    A(sk, PJ[1][:, :].rearrange("p (r k) -> p r k", r=4), ACT.Copy).then_inc(sk_ready.sem, 1)

                def peer_exp(h, tt):
                    act.wait_ge(top_ready.sem, top_ready.at(L, h * TT + (tt + 1)))
                    A(gnext[:, tt, :], gnext[:, tt, :], ACT.Exp, accum_out=psum16[:, tt:tt + 1])
                    A(small[:, 1023:1024], small[:, 1023:1024], ACT.Copy).then_inc(topexp_ready.sem, 1)
                    act.drain()

                def peer_weights(h, tt, more):
                    for k in range(TOPK):
                        n = tt * TOPK + k
                        act.wait_ge(dot_ready.sem, dot_ready.at(L, h * (TT * TOPK) + (n + 1)))
                        A(act_gelu[:, k:k + 1], act_dot[:, k:k + 1], ACT.Gelu_apprx_tanh)
                        act.drain()
                        A(act_w[:, k:k + 1], act_gelu[:, k:k + 1], ACT.Copy, scale=gcur[:, tt, k:k + 1])
                        act.drain()
                        if n >= 4:
                            act.wait_ge(row_used.sem, row_used.at(L, h * (TT * TOPK) + (n - 3)))
                        A(diag[:, k % 4, :], ident, ACT.Copy, scale=act_w[:, k:k + 1]).then_inc(diag_ready.sem, 1)
                        if k == 12 and more:
                            peer_exp(h + 1, tt)

                peer_out(0)
                peer_exp(0, 0)
                peer_exp(0, 1)
                with act.Fori(0, PH - 1) as h:
                    peer_out(h + 1)
                    for tt in range(TT):
                        peer_weights(h, tt, True)
                    act.wait_ge(row_used.sem, row_used.at(L, (h + 1) * (TT * TOPK)))
                    A(small[:, 1022:1023], small[:, 1022:1023], ACT.Copy)
                for tt in range(TT):
                    peer_weights(PH - 1, tt, False)
                act.drain()
            norm_root(ms_ready.at(depth, 1), 1)

        @block.vector
        def _(dve):
            V = nc.vector
            TS, TTn, STT = V.tensor_scalar, V.tensor_tensor, V.scalar_tensor_tensor

            def bc(ap, axis, shape):
                return ap.unsqueeze(axis).to_broadcast(shape)

            def norm(src, root_at, gain=None, extra=None):
                for tt in range(TT):
                    V.tensor_tensor_reduce(out=xn[:, tt, :], in0=src[:, tt, :], in1=src[:, tt, :], scale=1.0, scalar=0.0,
                                           op0=ALU.mult, op1=ALU.add, accum_out=ssq[:, tt:tt + 1])
                dve.drain()
                TS(ms, ssq, 1.0 / D, EPS, ALU.mult, ALU.add).then_inc(ms_ready.sem, 1)
                dve.wait_ge(root_ready.sem, root_at)
                V.reciprocal(rstd, root)
                dve.drain()
                for tt in range(TT):
                    if gain is None:
                        TS(xn[:, tt, :], src[:, tt, :], rstd[:, tt:tt + 1], None, ALU.mult).then_inc(xn_ready.sem, 1)
                    else:
                        i = STT(xn[:, tt, :], src[:, tt, :], rstd[:, tt:tt + 1], gain, ALU.mult, ALU.mult)
                        i.then_inc(xn_ready.sem, 1)

            def norm_T(full_at, dst, gain):
                for tt in range(TT):
                    for half in range(2):
                        dve.wait_ge(xT_full.sem, full_at(2 * tt + half + 1))
                        out = dst[:, 4 * half:4 * half + 4, tt * P:(tt + 1) * P]
                        src = M[2 * tt + half][:, :].rearrange("p (i t) -> p i t", i=4)
                        if gain is None:
                            i = V.tensor_copy(out, src)
                        else:
                            i = TTn(out, src, bc(gain[:, 4 * half:4 * half + 4], 2, [P, 4, P]), ALU.mult)
                        i.then_inc(hT_ready.sem, 1)

            V.memset(layer_base, 0.0)
            V.memset(small[:, 1022:1024], 0.0)
            dve.wait_ge(mem_in.sem, 16)
            norm(memN, 1)
            norm_T(lambda k: k, memT, None)
            dve.wait_ge(const_in.sem, 16)
            dve.wait_ge(x_in.sem, 16)

            def exp_exact(out, z):
                TS(e_n, z, 1.4426950408889634, MAGIC, ALU.mult, ALU.add)
                dve.drain()
                TS(e_n, e_n, MAGIC, -126.0, ALU.subtract, ALU.max)
                dve.drain()
                TS(e_n, e_n, 127.0, None, ALU.min)
                dve.drain()
                STT(e_f, e_n, -0.693359375, z, ALU.mult, ALU.add)
                dve.drain()
                STT(e_f, e_n, 2.12194440e-4, e_f, ALU.mult, ALU.add)
                TS(e_i[:, :], e_n, 127.0, 8388608.0, ALU.add, ALU.mult)
                dve.drain()
                TS(e_p, e_f, 1.0 / 5040, None, ALU.mult)
                for c in (1 / 720, 1 / 120, 1 / 24, 1 / 6, 0.5, 1.0):
                    dve.drain()
                    STT(e_p, e_p, c, e_f, ALU.add, ALU.mult)
                dve.drain()
                STT(out, e_p, 1.0, e_i[:, :].bitcast(F32), ALU.add, ALU.mult)
                dve.drain()

            def turns_of(out, z, rounded):
                TS(rounded, z, MAGIC, MAGIC, ALU.add, ALU.subtract)
                dve.drain()
                return TTn(out, z, rounded, ALU.subtract)

            def routing_halves(h, tt):
                for half in range(2):
                    r = 2 * tt + half
                    V.max(topv[:, r, 0:8], sk[:, r, :])
                dve.drain()
                for half in range(2):
                    r = 2 * tt + half
                    V.max_index(topi[:, r, 0:8], topv[:, r, 0:8], sk[:, r, :])
                    V.match_replace(skw[:, r, :], topv[:, r, 0:8], sk[:, r, :], -3e38)
                dve.drain()
                for half in range(2):
                    r = 2 * tt + half
                    V.max(topv[:, r, 8:16], skw[:, r, :])
                dve.drain()
                for half in range(2):
                    r = 2 * tt + half
                    V.max_index(topi[:, r, 8:16], topv[:, r, 8:16], skw[:, r, :])
                dve.drain()

            def routing_pairs(h, tt):
                a, b = 2 * tt, 2 * tt + 1
                c = cand[:, tt, :].rearrange("p (i j) -> p i j", i=16)
                TTn(c, bc(topv[:, a, :], 2, [P, 16, 16]), bc(topv[:, b, :], 1, [P, 16, 16]), ALU.add)
                V.tensor_copy(topf[:, a:b + 1, :], topi[:, a:b + 1, :])
                dve.drain()
                V.max(ctop[:, tt, 0:8], cand[:, tt, :])
                dve.drain()
                V.max_index(cpos[:, tt, 0:8], ctop[:, tt, 0:8], cand[:, tt, :])
                V.match_replace(candw[:, tt, :], ctop[:, tt, 0:8], cand[:, tt, :], -3e38)
                dve.drain()
                V.max(ctop[:, tt, 8:16], candw[:, tt, :])
                dve.drain()
                V.max_index(cpos[:, tt, 8:16], ctop[:, tt, 8:16], candw[:, tt, :])
                TS(gnext[:, tt, :], ctop[:, tt, :], ctop[:, tt, 0:1], None, ALU.subtract).then_inc(top_ready.sem, 1)
                dve.drain()

            def routing_experts(h, tt):
                TS(cab[:, 0, :], cpos[:, tt, :], 4, None, ALU.logical_shift_right)
                TS(cab[:, 1, :], cpos[:, tt, :], 15, None, ALU.bitwise_and)
                dve.drain()
                V.tensor_copy(cabf[:, :, :], cab[:, :, :])
                dve.drain()
                for w in range(2):
                    o = onehot[:, w, :].rearrange("p (k i) -> p k i", k=16)
                    TTn(o, bc(cabf[:, w, :], 2, [P, 16, 16]), bc(cst("iota"), 1, [P, 16, 16]), ALU.is_equal)
                dve.drain()
                for w in range(2):
                    o = onehot[:, w, :].rearrange("p (k i) -> p k i", k=16)
                    TTn(picked[:, w, :].rearrange("p (k i) -> p k i", k=16), o,
                        bc(topf[:, 2 * tt + w, :], 1, [P, 16, 16]), ALU.mult)
                dve.drain()
                V.tensor_reduce(eab[:, :, :], picked.rearrange("p w (k i) -> p w k i", k=16), AX.X, ALU.add)
                dve.drain()
                STT(eid[:, :], eab[:, 0, :], float(NKEYS), eab[:, 1, :], ALU.mult, ALU.add)
                dve.drain()
                TS(idx_next[:, tt, :], eid[:, :], layer_base, None, ALU.add)
                dve.drain()

            def publish(L, h, tt):
                dve.wait_ge(topexp_ready.sem, topexp_ready.at(L, h * TT + (tt + 1)))
                V.reciprocal(psum16[:, tt:tt + 1], psum16[:, tt:tt + 1])
                dve.drain()
                TS(gcur[:, tt, :], gnext[:, tt, :], psum16[:, tt:tt + 1], None, ALU.mult)
                V.tensor_copy(idx[:, tt, :], idx_next[:, tt, :]).then_inc(idx_ready.sem, 1)
                dve.drain()

            def peer_head(L, h, more):
                for tt in range(TT):
                    for k in range(TOPK):
                        n = tt * TOPK + k
                        s = k % SLOTS
                        dve.wait_ge(row_in[s].sem, row_in[s].at(L, h * (16 * TT * TOPK // SLOTS) + 16 * (n // SLOTS + 1)))
                        V.tensor_tensor_reduce(out=junk, in0=rows[:, s, 0:D], in1=xn[:, tt, :], scale=1.0, scalar=0.0,
                                               op0=ALU.mult, op1=ALU.add, accum_out=act_dot[:, k:k + 1]).then_inc(
                                                   dot_ready.sem, 1)
                        dve.drain()
                        if more and k == 3:
                            if tt == 0:
                                dve.wait_ge(sk_ready.sem, sk_ready.at(L, h + 2))
                                V.tensor_copy(eid[:, 0:1], layer_base)
                            routing_halves(h + 1, tt)
                        if more and k == 7:
                            routing_pairs(h + 1, tt)
                        if more and k == 11:
                            routing_experts(h + 1, tt)
                    for half in range(2):
                        c = slice(half * HALF, (half + 1) * HALF)
                        dve.wait_ge(row_used.sem, row_used.at(L, h * (TT * TOPK) + (tt + 1) * TOPK))
                        i = TTn(x[:, tt, c], x[:, tt, c], M[2 * tt + half][:, :], ALU.add)
                    i.then_inc(peer_added.sem, 1)
                    if more:
                        publish(L, h + 1, tt)

            with dve.Fori(0, depth) as L:
                dve.drain()
                norm(x, root_ready.at(L, 1))
                dve.wait_ge(par_in.sem, par_in.at(L, 16))
                norm_T(lambda k: xT_full.at(L, k), hT, pr("g_mix"))
                exp_exact(dts5, pr("ldt"))
                TTn(la, pr("lr"), dts5, ALU.mult)
                TTn(th, pr("li"), dts5, ALU.mult)
                dve.drain()
                TS(th2pi, th, 1.0 / (2 * math.pi), None, ALU.mult)
                dve.drain()
                turns_of(ang, th2pi, t16a)
                exp_exact(mag, la)
                V.tensor_copy(e_f, ang).then_inc(s5_arg.sem, 1)
                TTn(t16a, pr("lr"), pr("lr"), ALU.mult)
                TTn(t16b, pr("li"), pr("li"), ALU.mult)
                dve.drain()
                TTn(den, t16a, t16b, ALU.add)
                dve.drain()
                V.reciprocal(den, den)
                dve.wait_ge(s5_trig.sem, s5_trig.at(L, 1))
                TTn(ar, mag, cs16, ALU.mult)
                TTn(ai, mag, sn16, ALU.mult)
                dve.drain()
                TS(nr, ar, -1.0, None, ALU.add)
                dve.drain()
                TTn(wr, nr, pr("lr"), ALU.mult)
                TTn(t16a, ai, pr("li"), ALU.mult)
                TTn(wi, ai, pr("lr"), ALU.mult)
                TTn(t16b, nr, pr("li"), ALU.mult)
                dve.drain()
                TTn(wr, wr, t16a, ALU.add)
                TTn(wi, wi, t16b, ALU.subtract)
                dve.drain()
                TTn(wr, wr, den, ALU.mult)
                TTn(wi, wi, den, ALU.mult)
                dve.drain()

                def b3(ap):
                    return ap.rearrange("p (j i) -> p j i", i=16)
                wr3, wi3 = bc(wr, 2, [P, 16, 16]), bc(wi, 2, [P, 16, 16])
                bre, bim = b3(pr("bre")), b3(pr("bim"))
                TTn(b3(bb[:, 0, :]), bre, wr3, ALU.mult)
                TTn(b3(bb[:, 2, :]), bim, wi3, ALU.mult)
                TTn(b3(bb[:, 1, :]), bim, wr3, ALU.mult)
                dve.drain()
                TTn(bb[:, 0, :], bb[:, 0, :], bb[:, 2, :], ALU.subtract)
                dve.drain()
                TTn(b3(bb[:, 2, :]), bre, wi3, ALU.mult)
                dve.drain()
                TTn(bb[:, 1, :], bb[:, 1, :], bb[:, 2, :], ALU.add).then_inc(bb_ready.sem, 1)

                for G in range(KVH):
                    dve.wait_ge(score_full.sem, score_full.at(L, G + 1))
                    STT(sc0[:, 4 * G:4 * G + 4, :], M[G][:, :].rearrange("p (j k) -> p j k", j=4), HD ** -0.5,
                        bias[:, 4 * G:4 * G + 4, P:2 * P], ALU.mult, ALU.add)
                for G in range(KVH):
                    dve.wait_ge(score_full.sem, score_full.at(L, 3 + G))
                    for q in range(2):
                        hs = slice(4 * G + 2 * q, 4 * G + 2 * q + 2)
                        i = STT(sc1[:, hs, :], M[2 + 2 * G + q][:, :].rearrange("p (j k) -> p j k", j=2), HD ** -0.5,
                                bias[:, hs, :], ALU.mult, ALU.add)
                i.then_inc(score_read.sem, 1)
                dve.drain()
                for tt in range(TT):
                    V.tensor_reduce(mx[:, tt, :], (sc0, sc1)[tt], AX.X, ALU.max)
                dve.drain()
                for tt in range(TT):
                    TTn(mx[:, tt, :], mx[:, tt, :], pr("sinks"), ALU.max)
                dve.drain()
                for tt in range(TT):
                    TTn(sinkd[:, tt, :], pr("sinks"), mx[:, tt, :], ALU.subtract)
                    TS(nmx[:, tt, :], mx[:, tt, :], -1.0, None, ALU.mult).then_inc(max_ready.sem, 1)
                V.memset(xbcT[:, :, 0:3], 0.0)
                cw = pr("convw").rearrange("p (c k) -> p c k", k=4)
                dve.wait_ge(proj_free[1].sem, proj_free[1].at(L, 5))
                dve.wait_ge(proj_free[0].sem, proj_free[0].at(L, 5))
                V.tensor_copy(eid[:, 1:2], layer_base)
                dve.drain()
                for k in range(4):
                    for c in range(10):
                        src = xbcT[:, c, k:k + SEQ]
                        if k == 0:
                            TS(xbcC[:, c, :], src, cw[:, c, 0:1], pr("convb")[:, c:c + 1], ALU.mult, ALU.add)
                        else:
                            i = STT(xbcC[:, c, :], src, cw[:, c, k:k + 1], xbcC[:, c, :], ALU.mult, ALU.add)
                            if k == 3 and c in (4, 9):
                                i.then_inc(conv_ready.sem, 1)
                    dve.drain()
                for tt in range(TT):
                    dve.wait_ge(exp_ready.sem, exp_ready.at(L, tt + 1))
                    TTn(sums[:, tt, :], sums[:, tt, :], esink[:, tt, :], ALU.add)
                    dve.drain()
                    V.reciprocal(sums[:, tt, :], sums[:, tt, :])
                    dve.drain()
                    s = (sc0, sc1)[tt]
                    TTn(s, s, bc(sums[:, tt, :], 2, [P, HEADS, P * (tt + 1)]), ALU.mult).then_inc(p_ready.sem, 1)
                dve.wait_ge(dt_full.sem, dt_full.at(L, 1))
                TTn(dts, M[5][:, 0:32].rearrange("p (t h) -> p t h", t=TT), bc(pr("dtb"), 1, [P, TT, 16]), ALU.add)
                dve.drain()
                TS(sp_d, dts, -1.0, None, ALU.mult)
                dve.drain()
                TTn(sp_a, sp_d, dts, ALU.max).then_inc(dt_arg.sem, 1)
                TS(dts, dts, 0.0, None, ALU.max)
                dve.wait_ge(dt_exp.sem, dt_exp.at(L, 1))
                TS(sp_d, sp_e, 1.0, None, ALU.add).then_inc(dt_one.sem, 1)
                dve.drain()
                TS(sp_a, sp_d, -1.0, 1e-30, ALU.add, ALU.add)
                dve.wait_ge(dt_log.sem, dt_log.at(L, 1))
                TS(sp_l, sp_l, 1e-30, None, ALU.add)
                dve.drain()
                V.reciprocal(sp_a, sp_a)
                TTn(sp_l, sp_l, sp_e, ALU.mult)
                dve.drain()
                TTn(sp_l, sp_l, sp_a, ALU.mult)
                dve.drain()
                TTn(dts, dts, sp_l, ALU.add)
                dve.drain()
                STT(ad, dts, -1.0, bc(nega, 1, [P, TT, 16]), ALU.mult, ALU.mult).then_inc(ad_ready.sem, 1)

                def fractions(s):
                    dve.wait_ge(phi_ready.sem, phi_ready.at(L, s + 1))
                    turns_of(phi[:, s % 2, :], phi[:, s % 2, :], tmp1).then_inc(frac_ready.sem, 1)
                    dve.drain()

                def s5_out(c):
                    dve.wait_ge(y_full.sem, y_full.at(L, 2 * c + 2))
                    STT(uT[:, c, :], uT[:, c, :], pr("s5d")[:, c:c + 1], M[4 + c % 2][:, 0:SEQ], ALU.mult, ALU.add).then_inc(
                        ys5_pre.sem, 1)

                fractions(0)
                for s in range(8):
                    if s < 7:
                        fractions(s + 1)
                    b = s % 2
                    br, bi, S, C = M[2 * b][:, :], M[2 * b + 1][:, :], sn[:, b, :], cs[:, b, :]
                    dve.wait_ge(trig_ready.sem, trig_ready.at(L, s + 1))
                    dve.wait_ge(bu_full.sem, bu_full.at(L, s + 1))
                    TTn(rot_r, br, C, ALU.mult)
                    TTn(tmp1, br, S, ALU.mult)
                    TTn(tmp2, bi, S, ALU.mult)
                    TTn(rot_i, bi, C, ALU.mult).then_inc(bu_read.sem, 1)
                    dve.drain()
                    TTn(rot_r, rot_r, tmp2, ALU.add)
                    TTn(rot_i, rot_i, tmp1, ALU.subtract)
                    dve.drain()
                    for v in (rot_r, rot_i):
                        for i in range(2):
                            w = v[:, i * SEQ:(i + 1) * SEQ]
                            V.tensor_tensor_scan(w, mag[:, 2 * s + i:2 * s + i + 1].to_broadcast([P, SEQ]), w, 0.0,
                                                 ALU.mult, ALU.add)
                    if s >= 2:
                        dve.wait_ge(y_full.sem, y_full.at(L, s - 1))
                        V.tensor_copy(eid[:, 2:3], layer_base)
                    dve.drain()
                    TTn(xr_[:, b, :], rot_r, C, ALU.mult)
                    TTn(tmp1, rot_i, S, ALU.mult)
                    TTn(xi_[:, b, :], rot_r, S, ALU.mult)
                    TTn(tmp2, rot_i, C, ALU.mult)
                    dve.drain()
                    TTn(xr_[:, b, :], xr_[:, b, :], tmp1, ALU.subtract)
                    TTn(xi_[:, b, :], xi_[:, b, :], tmp2, ALU.add).then_inc(state_ready.sem, 1)
                    if s in (2, 4, 6):
                        s5_out(s // 2 - 1)
                    dve.drain()
                s5_out(3)

                def h3(ap):
                    return ap.rearrange("p (h d) -> p h d", h=SSDH)

                dve.wait_ge(cb_full.sem, cb_full.at(L, 1))
                TTn(cbm, M[5][:, :].rearrange("p (q l) -> p q l", q=4), bc(upto, 1, [P, 4, P]), ALU.mult).then_inc(
                    cb_ready.sem, 1)
                dve.drain()
                for c in range(2):
                    if c == 1:
                        dve.wait_ge(diff_full.sem, diff_full.at(L, 4))
                    TTn(adU, bc(ad[:, c, :], 2, [P, SSDH, P]), bc(upto, 1, [P, SSDH, P]), ALU.mult).then_inc(
                        adU_ready.sem, 1)
                    dve.wait_ge(xs_ready.sem, xs_ready.at(L, 2 * c + 2))
                    TTn(h3(xdt[:, c, :]), h3(xsn[:, c, :]), bc(dts[:, c, :], 2, [P, SSDH, HD]), ALU.mult)
                    TTn(h3(ytmp), h3(xsn[:, c, :]), bc(pr("ssdd"), 2, [P, SSDH, HD]), ALU.mult)
                    if c == 0:
                        dve.drain()
                        dve.wait_ge(misc_ready.sem, misc_ready.at(L, 1))
                        TTn(h3(xdec), h3(xdt[:, 0, :]), bc(dec0, 2, [P, SSDH, HD]), ALU.mult).then_inc(xdec_ready.sem, 1)
                    if c == 1:
                        for i in range(4):
                            dve.wait_ge(proj_full.sem, proj_full.at(L, J_ATTN + i + 1))
                            TTn(mergedT[:, 2 * i:2 * i + 2, :], PJ[(J_ATTN + i) % 2][:, :].rearrange(
                                "p (a t) -> p a t", a=2), gT[:, 2 * i:2 * i + 2, :], ALU.mult).then_inc(
                                    proj_free[(J_ATTN + i) % 2].sem, 1)
                    dve.wait_ge(decay_ready.sem, decay_ready.at(L, 4 * c + 4))
                    for g in range(2):
                        v = decayE[:, 8 * g:8 * g + 8, :]
                        i = TTn(v, v, bc(cbm[:, 2 * c + g, :], 1, [P, 8, P]), ALU.mult)
                    i.then_inc(w_ready.sem, 1)
                    dve.wait_ge(yd_full.sem, yd_full.at(L, c + 1))
                    for half in range(2):
                        q = slice(half * HALF, (half + 1) * HALF)
                        i = TTn(xn[:, c, q], ytmp[:, q], M[4 + half][:, :], ALU.add)
                    i.then_inc(yd_read.sem, 1)
                    dve.drain()
                    if c == 1:
                        dve.wait_ge(yo_full.sem, yo_full.at(L, 1))
                        for g in range(2):
                            q = slice(g * HALF, (g + 1) * HALF)
                            TTn(ytmp[:, q].rearrange("p (h d) -> p h d", h=8), M[g][:, :].rearrange(
                                "p (h d) -> p h d", h=8), bc(eac1[:, 8 * g:8 * g + 8], 2, [P, 8, HD]), ALU.mult)
                        dve.drain()
                        TTn(xn[:, 1, :], xn[:, 1, :], ytmp, ALU.add)
                        dve.drain()
                TTn(zs[:, :, :], xn[:, :, :], zs[:, :, :], ALU.mult)
                for i in range(4):
                    dve.wait_ge(sg_ready.sem, sg_ready.at(L, i + 1))
                    dve.wait_ge(proj_full.sem, proj_full.at(L, J_GLU + 2 * i + 1))
                    TTn(ytmp[:, 0:HALF], PJ[0][:, :], sgate[:, i % 2, :], ALU.mult).then_inc(proj_free[0].sem, 1)
                    dve.drain()
                    TTn(ytmp[:, 0:HALF].rearrange("p (a t) -> p a t", a=2), ytmp[:, 0:HALF].rearrange(
                        "p (a t) -> p a t", a=2), gT[:, 8 + 2 * i:10 + 2 * i, :], ALU.mult).then_inc(sg_used.sem, 1)
                    dve.drain()
                    TTn(mergedT[:, 2 * i:2 * i + 2, :], mergedT[:, 2 * i:2 * i + 2, :],
                        ytmp[:, 0:HALF].rearrange("p (a t) -> p a t", a=2), ALU.add)
                    dve.drain()
                norm(zs, root_ready.at(L, 2))
                norm_T(lambda k: xT_full.at(L, 4 + k), hT, pr("g_ssd"))
                for i in range(4):
                    dve.wait_ge(proj_full.sem, proj_full.at(L, J_SSD + i + 1))
                    yv = ytmp[:, 0:HALF].rearrange("p (a t) -> p a t", a=2)
                    TTn(yv, PJ[(J_SSD + i) % 2][:, :].rearrange("p (a t) -> p a t", a=2),
                        gT[:, 16 + 2 * i:18 + 2 * i, :], ALU.mult).then_inc(proj_free[(J_SSD + i) % 2].sem, 1)
                    dve.drain()
                    last = TTn(mergedT[:, 2 * i:2 * i + 2, :], mergedT[:, 2 * i:2 * i + 2, :], yv, ALU.add)
                    if i < 3:
                        dve.drain()
                last.then_inc(merged_ready.sem, 1)

                def add_to_x(j, tt, c):
                    dve.wait_ge(proj_full.sem, proj_full.at(L, j + 1))
                    q = slice(c * HALF, (c + 1) * HALF)
                    TTn(x[:, tt, q], x[:, tt, q], PJ[j % 2][:, :], ALU.add).then_inc(proj_free[j % 2].sem, 1)

                for c in range(2):
                    for tt in range(TT):
                        add_to_x(J_WO + 2 * c + tt, tt, c)
                dve.drain()
                norm(x, root_ready.at(L, 3))
                norm_T(lambda k: xT_full.at(L, 8 + k), hT, pr("g_x"))
                for tt in range(TT):
                    dve.wait_ge(sx_full.sem, sx_full.at(L, tt + 1))
                    for q in range(2):
                        V.tensor_reduce(sumx[:, tt, 2 * q:2 * q + 2],
                                        M[2 * tt + q][:, :].rearrange("p (a k) -> p a k", a=2), AX.X, ALU.max)
                    dve.drain()
                    TS(mxx[:, tt, :], sumx[:, tt, :], -HD ** -0.5, None, ALU.mult).then_inc(mxx_ready.sem, 1)
                for tt in range(TT):
                    dve.wait_ge(expx_ready.sem, expx_ready.at(L, tt + 1))
                    V.reciprocal(sumx[:, tt, :], sumx[:, tt, :])
                    dve.drain()
                    TTn(scx[:, tt, :, :], scx[:, tt, :, :], bc(sumx[:, tt, :], 2, [P, XH, SEQ]), ALU.mult).then_inc(
                        px_ready.sem, 1)
                for tt in range(TT):
                    for c in range(2):
                        add_to_x(J_XO + 2 * tt + c, tt, c)
                dve.drain()
                dve.wait_ge(gnat_in.sem, gnat_in.at(L, 16))
                V.tensor_copy(eid[:, 3:4], layer_base)
                norm(x, root_ready.at(L, 4), gain=gnat)
                norm_T(lambda k: xT_full.at(L, 12 + k), hT, None)
                dve.wait_ge(sk_ready.sem, sk_ready.at(L, 1))
                V.tensor_copy(eid[:, 0:1], layer_base).then_inc(hn_ready.sem, 1)
                for tt in range(TT):
                    routing_halves(0, tt)
                    routing_pairs(0, tt)
                    routing_experts(0, tt)
                    publish(L, 0, tt)
                with dve.Fori(0, PH - 1) as h:
                    peer_head(L, h, True)
                    dve.drain()
                peer_head(L, PH - 1, False)
                dve.drain()
                TS(layer_base, layer_base, float(EXPERTS), None, ALU.add)
                dve.drain()
            dve.wait_ge(gnat_in.sem, gnat_in.at(depth, 16))
            V.tensor_copy(eid[:, 0:1], layer_base)
            norm(x, root_ready.at(depth, 1), gain=gnat)


def constants():
    c = np.zeros((P, NCONST), np.float32)

    def put(name, v):
        c[:, CCOLS[name][0]:CCOLS[name][1]] = v
    i = np.arange(P)
    put("ident", np.eye(P))
    put("later", i[:, None] > i[None, :])
    put("upto", i[:, None] <= i[None, :])
    dist = i[:, None] - np.arange(2 * P)[None, :] + P
    slopes = 2.0 ** (-8.0 * (np.arange(HEADS) + 1.0) / HEADS)
    b = np.where((dist >= 0) & (dist < P), 0, 1)[:, None, :] * NEG - slopes[None, :, None] * np.where(
        (dist >= 0) & (dist < P), dist, 0)[:, None, :]
    put("bias", b.reshape(P, -1))
    put("time", np.arange(SEQ)[None, :])
    put("iota", np.arange(16)[None, :])
    return c


def lay_out(a, depth):
    f = lambda n: np.asarray(a[n])[:depth]
    w_in = f("w_in")
    L = depth

    def tiles(w):
        l, k, n = w.shape
        return w.reshape(l, k // P, P, n // P, P).transpose(0, 3, 2, 1, 4)

    def by_tiles(w, per):
        t = tiles(w)
        l, n, p, k, c = t.shape
        return t.reshape(l, n // per, per, p, k * c).transpose(0, 1, 3, 2, 4).reshape(l, n // per, P, UNIT)

    def by_rows(w, kts, cols):
        l, k, n = w.shape
        t = w.reshape(l, k // (kts * P), kts, P, n // cols, cols).transpose(0, 4, 1, 3, 2, 5)
        return t.reshape(l, -1, P, UNIT)

    q = w_in[:, :, 0:512].reshape(L, D, KVH, REP, HD).transpose(0, 1, 3, 2, 4).reshape(L, D, 512)
    k, v = w_in[:, :, 512:640], w_in[:, :, 640:768]
    u, z, xbc = w_in[:, :, 768:1280], w_in[:, :, 1280:2304], w_in[:, :, 2304:3584]
    wdt, gat = w_in[:, :, 3584:3600], w_in[:, :, 3600:6672]
    wao = f("w_attn_out").reshape(L, KVH, REP, HD, D).transpose(0, 2, 1, 3, 4).reshape(L, 512, D)
    wkv = f("xa_wkv")
    glu_a, glu_b = by_tiles(f("s5_glu_a"), 4), by_tiles(f("s5_glu_b"), 4)
    units = np.concatenate([
        by_tiles(np.concatenate([q, k, v, u, xbc], 2), 2), by_rows(z, 4, 512), by_tiles(gat, 2), by_tiles(wao, 4),
        by_tiles(wkv[:, :, :256], 2), by_rows(wkv[:, :, 256:], 8, 256),
        glu_a[:, 0:1], glu_b[:, 0:1], glu_a[:, 1:2], glu_b[:, 1:2],
        by_tiles(f("w_ssd_out"), 2), by_rows(f("w_o"), 4, 512), by_tiles(f("xa_wq"), 2), by_rows(f("xa_wo"), 2, 1024),
    ], 1)
    assert units.shape[1] == UNITS
    units = np.concatenate([units.reshape(L * UNITS, P, UNIT), np.zeros((RING, P, UNIT), np.float32)])
    wq = f("peer_wq")
    wq = wq.reshape(L, KT, P, PH, 256).transpose(0, 3, 2, 1, 4).reshape(L * PH, P, UNIT)

    par = np.zeros((L + 1, P, NPAR), np.float32)

    def put(name, val):
        par[:L, :, COLS[name][0]:COLS[name][1]] = val.reshape(L, -1, COLS[name][1] - COLS[name][0])

    def states(t):
        r = t.reshape((L, 16, P) + t.shape[3:])
        return np.moveaxis(r, 1, 2)

    def chans(t):
        return t.reshape(L, -1, P).transpose(0, 2, 1)
    put("lr", states(f("s5_lambda_re")))
    put("li", states(f("s5_lambda_im")))
    put("ldt", states(np.repeat(f("s5_log_dt")[:, :, None], 64, 2)))
    put("bre", states(f("s5_b_re")))
    put("bim", states(f("s5_b_im")))
    put("cre", states(f("s5_c_re").transpose(0, 1, 3, 2)))
    put("cim", states(f("s5_c_im").transpose(0, 1, 3, 2)))
    put("s5d", chans(f("s5_d")))
    put("convw", f("ssd_conv_w").reshape(L, 4, 10, P).transpose(0, 3, 2, 1))
    put("convb", chans(f("ssd_conv_b")))
    for n, s in (("g_mix", "norm_mix"), ("g_x", "norm_xattn"), ("g_mem", "norm_mem"), ("g_ssd", "ssd_norm")):
        put(n, chans(f(s)))
    for n, s in (("dtb", "ssd_dt_bias"), ("alog", "ssd_a_log"), ("ssdd", "ssd_d"), ("sinks", "attn_sinks")):
        put(n, np.repeat(f(s)[:, None, :], P, 1))
    put("wdt", wdt.reshape(L, KT, P, 16).transpose(0, 2, 1, 3))
    put("k1", f("peer_k1").transpose(0, 2, 1))
    put("k2", f("peer_k2").transpose(0, 2, 1))
    table = np.concatenate([f("peer_u"), f("peer_v")], 2).reshape(L * EXPERTS, ROW)
    return {"x": np.asarray(a["x"]), "mem": np.asarray(a["mem"]), "units": units, "wq": wq, "par": par,
            "const": constants(), "g_ffn": f("norm_ffn"), "g_final": np.asarray(a["norm_final"]), "table": table}


def program(nc, arrays, depth):
    aps = [nc.dram_tensor(f"in_{n}", v.shape, F32, kind="ExternalInput").ap() for n, v in arrays.items()]
    out = nc.dram_tensor("out", (1, SEQ, D), F32, kind="ExternalOutput").ap()
    build(nc, depth, *aps, out)


def kernel(**inputs):
    import concourse.bacc as bacc
    from concourse.bass_utils import run_bass_kernel_spmd

    depth = inputs["norm_mix"].shape[0]
    arrays = {k: np.ascontiguousarray(v) for k, v in lay_out(inputs, depth).items()}
    nc = bacc.Bacc("TRN2", target_bir_lowering=False, num_devices=1)
    program(nc, arrays, depth)
    r = run_bass_kernel_spmd(nc, [{f"in_{k}": v for k, v in arrays.items()}], core_ids=[0])
    return r.results[0]["out"]
```

```python
from contextlib import ExitStack
import math

import numpy as np
import concourse.bass as bass
from concourse import mybir
from concourse.alu_op_type import AluOpType as ALU

F32, F32R, U32, I32 = mybir.dt.float32, mybir.dt.float32r, mybir.dt.uint32, mybir.dt.int32
ACT = mybir.ActivationFunctionType
AX = mybir.AxisListType

P = 128
D = 1024
SEQ = 256
TT = SEQ // P
KT = D // P
HALF = 512
EPS = 1e-6
HEADS, KVH, REP, HD = 8, 2, 4, 64
S5W, S5TILES = 512, 16
SSDH = 16
XH = 4
PH, TOPK, NKEYS = 8, 16, 128
EXPERTS = NKEYS * NKEYS
MAGIC = 12582912.0
TWO_PI = 6.283185
FAR = 1e30

UNIT = 1024
RING = 4
U_QKVUX, U_XK, U_XV, U_Z, U_GAB, U_ATTN, U_GC, U_GLU, U_SSD, U_WO, U_XQ, U_XO = (
    0, 20, 22, 24, 32, 48, 52, 60, 68, 76, 84, 86)
UNITS = 88
J_QKVUX, J_XK, J_XV, J_Z, J_GAB, J_ATTN, J_GC, J_GLU, J_SSD, J_WO, J_XQ, J_XO = (
    0, 10, 11, 12, 16, 24, 28, 32, 40, 44, 48, 49)
JOBS = 53
UNITS_OF_JOB = ([2 * n + 2 for n in range(10)] + [22, 24] + [28, 28, 32, 32] + [34 + 2 * n for n in range(8)]
                + [49, 50, 51, 52] + [54, 56, 58, 60] + [61 + n for n in range(8)] + [70, 72, 74, 76]
                + [80, 80, 84, 84] + [86] + [87, 87, 88, 88])

COLS = {}
_at = 0
for _name, _n in (("lr", 16), ("li", 16), ("ldt", 16), ("bre", 256), ("bim", 256), ("cre", 256), ("cim", 256),
                  ("s5d", 4), ("convw", 40), ("convb", 10), ("g_mix", 8), ("g_x", 8), ("g_mem", 8), ("g_ssd", 8),
                  ("dtb", 16), ("alog", 16), ("ssdd", 16), ("sinks", 8), ("wdt", 128), ("k1", 128), ("k2", 128)):
    COLS[_name] = (_at, _at + _n)
    _at += _n
NPAR = _at
CCOLS = {}
_at = 0
for _name, _n in (("ident", 128), ("later", 128), ("upto", 128), ("dist", 256), ("time", 256), ("iota", 16)):
    CCOLS[_name] = (_at, _at + _n)
    _at += _n
NCONST = _at

SLOTS = 8
ROW = 2 * D


class Signal:

    def __init__(self, sem, per, pre=0):
        self.sem, self.per, self.pre = sem, per, pre

    def at(self, layer, k):
        return layer * self.per + (k + self.pre)


def build(nc, depth, x_d, mem_d, units_d, wq_d, par_d, const_d, gffn_d, gfin_d, table_d, memT_d, out_d):
    ctx = ExitStack()
    with ctx:
        def sb(name, shape, dt=F32):
            return ctx.enter_context(nc.sbuf_tensor(name, shape, dt))

        def sig(name, per, pre=0):
            return Signal(ctx.enter_context(nc.semaphore(name)), per, pre)

        const = sb("const", [P, NCONST])
        par = sb("par", [P, NPAR])
        x = sb("x", [P, TT, D])
        xn = sb("xn", [P, TT, D])
        ring = sb("ring", [P, RING, UNIT])
        w_hi, w_lo = sb("w_hi", [P, RING, UNIT], F32R), sb("w_lo", [P, RING, UNIT], F32R)
        h_hi, h_lo = sb("h_hi", [P, KT, SEQ], F32R), sb("h_lo", [P, KT, SEQ], F32R)
        b_hi, b_lo = sb("b_hi", [P, KT, SEQ], F32R), sb("b_lo", [P, KT, SEQ], F32R)
        wdt_hi, wdt_lo = sb("wdt_hi", [P, P], F32R), sb("wdt_lo", [P, P], F32R)
        arena = sb("arena", [P, SLOTS * ROW])
        gates = sb("gates", [P, 16 * SEQ])
        zs = sb("zs", [P, TT, D])
        uT = sb("uT", [P, 4, SEQ])
        gnat = uT[:, :, :].rearrange("p a b -> p (a b)")
        kvx = sb("kvx", [P, 2 * HALF])
        small = sb("small", [P, 800])

        def cst(name):
            return const[:, CCOLS[name][0]:CCOLS[name][1]]

        def pr(name):
            return par[:, COLS[name][0]:COLS[name][1]]

        def cut(t, start, *shape):
            n = int(np.prod(shape))
            v = t[:, start:start + n]
            if len(shape) == 2:
                v = v.rearrange("p (a b) -> p a b", b=shape[1])
            if len(shape) == 3:
                v = v.rearrange("p (a b c) -> p a b c", b=shape[1], c=shape[2])
            return v

        ident, later, upto = cst("ident"), cst("later"), cst("upto")

        sc0, sc1 = cut(gates, 0, HEADS, P), cut(gates, 1024, HEADS, 2 * P)
        pT0 = cut(gates, 3072, HEADS * P)
        pT1 = cut(arena, 8992, TT, HEADS * P)
        gT = cut(gates, 0, 16, SEQ)
        qT, kT, vN = cut(arena, 4896, REP, SEQ), cut(arena, 5920, SEQ), cut(arena, 2048, TT, P)
        kxT, vx = cut(kvx, 0, 2, SEQ), cut(kvx, HALF, TT, SEQ)
        Zr, Zi, Cr, Ci = (cut(arena, 512 * i, S5TILES, 32) for i in range(4))
        Zflat = [cut(arena, 512 * i, 4 * P) for i in range(2)]
        xbcT, xbcC = cut(arena, 2304, 10, SEQ + 3), cut(arena, 13824, 10, SEQ)
        bb = cut(arena, 15136, 3, 256)
        S5N = 4 * SEQ
        rot_r, rot_i, tmp1, tmp2 = (cut(arena, 4896 + i * S5N, 4, SEQ) for i in range(4))
        sn, cs = [cut(arena, 8992 + i * S5N, 4, SEQ) for i in (0, 2)], [cut(arena, 8992 + i * S5N, 4, SEQ) for i in (1, 3)]
        phi, turn = cut(arena, 13088, 4, SEQ), cut(arena, 14112, 4, SEQ)
        xflat = xn[:, :, :].rearrange("p a b -> p (a b)")
        memT = cut(xflat, 0, KT, SEQ)
        xr_, xi_ = cut(xflat, 0, 4, SEQ), cut(xflat, S5N, 4, SEQ)
        xsn, xdt = cut(arena, 0, TT, D), cut(arena, 2048, TT, D)
        adU, decayE = cut(arena, 4096, SSDH, P), cut(arena, 6144, SSDH, P)
        xdec, bN, s0 = cut(arena, 8192, D), cut(arena, 9216, P), cut(arena, 9344, HALF)
        cbm, ytmp = cut(arena, 9856, 4, P), cut(arena, 10368, D)
        sgate = cut(arena, 8192, 2, HALF)
        mergedT = cut(arena, 11392, KT, SEQ)
        memN = cut(arena, 0, TT, D)
        memT0 = cut(arena, 2048, KT, SEQ)
        qxT = cut(arena, 0, 2, SEQ)
        scx, pTx = cut(arena, 1024, TT, XH, SEQ), cut(arena, 3072, TT, XH, TT * P)
        wq = zs[:, :, :].rearrange("p a b -> p (a b)").rearrange("p (k c) -> p k c", k=TT)
        rows = arena[:, :].rearrange("p (s r) -> p s r", s=SLOTS)
        qh = cut(gates, 0, 2, SEQ)
        sk, skw = cut(gates, 512, 2 * TT, NKEYS), cut(gates, 1024, 2 * TT, NKEYS)
        cand, candw = cut(gates, 1536, TT, 256), cut(gates, 2048, TT, 256)
        onehot, picked = cut(gates, 2560, 2, 256), cut(gates, 3072, 2, 256)
        diag = cut(gates, 3584, 4, P)
        junk = cut(kvx, 0, D)

        _free = [0]

        def tiny(*shape):
            n = int(np.prod(shape))
            _free[0] += n
            assert _free[0] <= 798
            return cut(small, _free[0] - n, *shape)

        ssq, ms, root, rstd = tiny(2), tiny(2), tiny(2), tiny(2)
        mx, nmx, sums, sinkd, esink = tiny(2, 8), tiny(2, 8), tiny(2, 8), tiny(2, 8), tiny(2, 8)
        dts5, la, th, mag, ar, ai, nr, den, wr, wi, t16a, t16b, th2pi = (tiny(16) for _ in range(13))
        ang, e_n, e_f, e_p, sn16, cs16, hs16 = (tiny(16) for _ in range(7))
        dts, ad, sp_a, sp_e, sp_l, sp_d = (tiny(TT, 16) for _ in range(6))
        nega, dec0, eac1 = tiny(16), tiny(16), tiny(16)
        mxx, sumx = tiny(2, 4), tiny(2, 4)
        act_dot, act_gelu, act_w = tiny(16), tiny(16), tiny(16)
        gcur, gnext = tiny(TT, 16), tiny(TT, 16)
        psum16 = tiny(2)
        layer_base = tiny(1)
        e_i = sb("e_i", [P, 16], I32)
        topv = sb("topv", [P, 2 * TT, 16])
        topi = sb("topi", [P, 2 * TT, 16], U32)
        topf = sb("topf", [P, 2 * TT, 16])
        ctop = sb("ctop", [P, TT, 16])
        cpos = sb("cpos", [P, TT, 16], U32)
        cab = sb("cab", [P, 2, 16], U32)
        cabf = sb("cabf", [P, 2, 16])
        eab = sb("eab", [P, 2, 16])
        eid = sb("eid", [P, 16])
        idx_next = sb("idx_next", [P, TT, 16], U32)
        idx = sb("idx", [P, TT, 16], U32)

        psum = ctx.enter_context(nc.psum_tensor("psum", [P, 8, HALF], F32))
        PJ, M = [psum[:, i, :] for i in range(2)], [psum[:, i, :] for i in range(2, 8)]

        const_in = sig("const_in", 0, 0)
        x_in, mem_in = sig("x_in", 0), sig("mem_in", 0)
        par_in = sig("par_in", 16)
        gnat_in = sig("gnat_in", 16)
        unit_in = [sig(f"unit_in{r}", 16 * UNITS // RING) for r in range(RING)]
        wq_in = sig("wq_in", 16 * PH)
        row_in = [sig(f"row_in{s}", 16 * PH * TT * TOPK // SLOTS) for s in range(SLOTS)]
        out_done = sig("out_done", 0)
        ms_ready, root_ready = sig("ms_ready", 4, 1), sig("root_ready", 4, 1)
        xn_ready = sig("xn_ready", 8, 2)
        xT_full, hT_ready = sig("xT_full", 16, 4), sig("hT_ready", 16, 4)
        hi_ready, lo_ready, unit_used = sig("hi_ready", UNITS), sig("lo_ready", UNITS), sig("unit_used", UNITS)
        proj_free = [sig("proj_free0", 27), sig("proj_free1", 26)]
        score_full, score_read = sig("score_full", 4), sig("score_read", 1)
        max_ready, exp_ready, p_ready = sig("max_ready", 2), sig("exp_ready", 2), sig("p_ready", 2)
        pT_full, pT_ready = sig("pT_full", 6), sig("pT_ready", 6)
        o_full, oT_ready = sig("o_full", 2), sig("oT_ready", 2)
        memT_in, hm_ready, wdt_ready = sig("memT_in", 16), sig("hm_ready", 1), sig("wdt_ready", 1)
        wdt_rounded = sig("wdt_rounded", 1)
        memT_made, memT_out = sig("memT_made", 0), sig("memT_out", 0)
        s5_arg, s5_trig = sig("s5_arg", 1, 1), sig("s5_trig", 1, 1)
        bb_ready, frames_ready = sig("bb_ready", 1), sig("frames_ready", 1)
        zT_full, zT_ready = sig("zT_full", 2), sig("zT_ready", 2)
        phi_ready, frac_ready, trig_ready = sig("phi_ready", 4), sig("frac_ready", 4), sig("trig_ready", 4)
        bu_full, bu_read, state_ready, y_full = sig("bu_full", 4), sig("bu_read", 4), sig("state_ready", 4), sig("y_full", 4)
        ys5_pre, ys5_gelu, ys5_ready = sig("ys5_pre", 4), sig("ys5_gelu", 1), sig("ys5_ready", 1)
        conv_ready, silu_ready = sig("conv_ready", 2), sig("silu_ready", 2)
        dt_full, dt_arg, dt_exp, dt_one, dt_log, ad_ready = (sig(n, 1) for n in (
            "dt_full", "dt_arg", "dt_exp", "dt_one", "dt_log", "ad_ready"))
        xs_full, xs_ready = sig("xs_full", 4), sig("xs_ready", 4)
        misc_full, misc_ready = sig("misc_full", 1), sig("misc_ready", 1)
        cb_full, cb_ready = sig("cb_full", 1), sig("cb_ready", 1)
        adU_ready, diff_full, decay_ready = sig("adU_ready", 2), sig("diff_full", 8), sig("decay_ready", 8)
        w_ready, xdec_ready, yd_full, yd_read = sig("w_ready", 2), sig("xdec_ready", 1), sig("yd_full", 2), sig("yd_read", 2)
        s0_full, s0_ready, yo_full = sig("s0_full", 1), sig("s0_ready", 1), sig("yo_full", 1)
        sg_used = sig("sg_used", 4)
        merged_ready = sig("merged_ready", 1)
        sx_full, mxx_ready, expx_ready, px_ready = sig("sx_full", 2), sig("mxx_ready", 2), sig("expx_ready", 2), sig("px_ready", 2)
        pTx_full, pTx_ready, ox_full, ox_ready = sig("pTx_full", 4), sig("pTx_ready", 4), sig("ox_full", 2), sig("ox_ready", 2)
        hn_ready = sig("hn_ready", 1)
        wq_hi, wq_lo = sig("wq_hi", PH), sig("wq_lo", PH)
        qh_full, qh_ready = sig("qh_full", PH), sig("qh_ready", PH)
        sk_full, sk_ready = sig("sk_full", PH), sig("sk_ready", PH)
        top_ready, topexp_ready = sig("top_ready", PH * TT), sig("topexp_ready", PH * TT)
        idx_ready = sig("idx_ready", PH * TT)
        dot_ready = sig("dot_ready", PH * TT * TOPK)
        diag_ready = sig("diag_ready", PH * TT * TOPK)
        row_used = sig("row_used", PH * TT * TOPK)
        peer_added = sig("peer_added", PH * TT)
        gather_go = sig("gather_go", 0)
        routed = sig("routed", PH)

        block = ctx.enter_context(nc.Block())

        @block.sync
        def _(sp):
            sp.dma_start(par[:, :], par_d[0]).then_inc(par_in.sem, 16)
            sp.dma_start(arena[:, 0:TT * D].rearrange("p (t d) -> p t d", t=TT),
                         mem_d.rearrange("b (t p) d -> p (b t) d", p=P)).then_inc(mem_in.sem, 16)
            sp.dma_start(x[:, :, :], x_d.rearrange("b (t p) d -> p (b t) d", p=P)).then_inc(x_in.sem, 16)
            sp.dma_start(const[:, :], const_d).then_inc(const_in.sem, 16)
            for n in range(RING):
                sp.dma_start(ring[:, n, :], units_d[n]).then_inc(unit_in[n].sem, 16)
            sp.wait_ge(memT_made.sem, 1)
            sp.dma_start(memT_d.rearrange("p (k t) -> p k t", k=KT), memT0).then_inc(memT_out.sem, 16)
            sp.wait_ge(memT_out.sem, 16)
            with sp.Fori(0, depth) as L:
                sp.wait_ge(hT_ready.sem, hT_ready.at(L, 4))
                sp.dma_start(memT, memT_d.rearrange("p (k t) -> p k t", k=KT)).then_inc(memT_in.sem, 16)
                for n in range(UNITS):
                    sp.wait_ge(lo_ready.sem, lo_ready.at(L, n + 1))
                    sp.dma_start(ring[:, n % RING, :], units_d[L * UNITS + (n + RING)]).then_inc(
                        unit_in[n % RING].sem, 16)
                    if n == U_SSD:
                        sp.wait_ge(xn_ready.sem, xn_ready.at(L, 4))
                        sp.dma_start(gnat, gffn_d[L].partition_broadcast(P)).then_inc(gnat_in.sem, 16)
                        sp.dma_start(wq, wq_d[L * PH].rearrange("p (k c) -> p k c", k=TT)).then_inc(wq_in.sem, 16)
                with sp.Fori(1, PH) as h:
                    sp.wait_ge(wq_lo.sem, wq_lo.at(L, h))
                    sp.dma_start(wq, wq_d[L * PH + h].rearrange("p (k c) -> p k c", k=TT)).then_inc(
                        wq_in.sem, 16)
                sp.wait_ge(sk_full.sem, sk_full.at(L, PH))
                sp.dma_start(par[:, :], par_d[L + 1]).then_inc(par_in.sem, 16)
            sp.wait_ge(hn_ready.sem, depth)
            sp.dma_start(gnat, gfin_d.partition_broadcast(P)).then_inc(gnat_in.sem, 16)
            sp.wait_ge(xn_ready.sem, xn_ready.at(depth, 2))
            sp.dma_start(out_d.rearrange("b (t p) d -> p (b t) d", p=P), xn[:, :, :]).then_inc(out_done.sem, 16)
            sp.wait_ge(out_done.sem, 16)
            for n in range(RING):
                sp.wait_ge(unit_in[n].sem, unit_in[n].per * depth + 16)
            sp.wait_ge(par_in.sem, 16 * (depth + 1))

        @block.gpsimd
        def _(pool):

            def gathers(L, h, first):
                for tt in range(TT):
                    pool.wait_ge(idx_ready.sem, idx_ready.at(L, h * TT + (tt + 1)))
                    nc.gpsimd.sem_inc(gather_go.sem, 1)
                    for k in range(TOPK):
                        if not (first and tt == 0 and k < SLOTS):
                            pool.wait_ge(row_used.sem, row_used.at(L, h * (TT * TOPK) + (tt * TOPK + k + 1 - SLOTS)))
                            nc.gpsimd.sem_inc(gather_go.sem, 1)
                        pool.indirect_dma_start(
                            out=rows[:, k % SLOTS, :], out_offset=None, in_=table_d,
                            in_offset=bass.IndirectOffsetOnAxis(ap=idx[:, tt, k:k + 1], axis=0),
                        ).then_inc(row_in[k % SLOTS].sem, 16)

            def into_tiles(dst, src, scale):
                for g in range(2):
                    last = nc.gpsimd.tensor_scalar(
                        dst[64 * g:64 * g + 64, :, 16 * g:16 * g + 16],
                        src.rearrange("p (j i) -> p j i", i=16)[64 * g:64 * g + 64, :, :], scale, 0.0, ALU.mult, ALU.add)
                return last

            with pool.Fori(0, depth) as L:
                def weights_lo(n0, n1):
                    for n in range(n0, n1):
                        pool.wait_ge(hi_ready.sem, hi_ready.at(L, n + 1))
                        nc.gpsimd.tensor_tensor(w_lo[:, n % RING, :], ring[:, n % RING, :],
                                                w_hi[:, n % RING, :].bitcast(F32), ALU.subtract).then_inc(lo_ready.sem, 1)

                weights_lo(0, 2)
                pool.wait_ge(par_in.sem, par_in.at(L, 16))
                pool.wait_ge(hT_ready.sem, hT_ready.at(L, 4))
                nc.gpsimd.sem_inc(gather_go.sem, 1)
                nc.gpsimd.memset(arena[:, 0:2048], 0.0)
                pool.drain()
                weights_lo(2, 6)
                pool.drain()
                into_tiles(Cr, pr("cre"), 1.0)
                into_tiles(Ci, pr("cim"), -1.0)
                pool.drain()
                weights_lo(6, 8)
                pool.wait_ge(bb_ready.sem, bb_ready.at(L, 1))
                nc.gpsimd.sem_inc(gather_go.sem, 1)
                pool.drain()
                into_tiles(Zr, bb[:, 0, :], 1.0)
                into_tiles(Zi, bb[:, 1, :], 1.0).then_inc(frames_ready.sem, 1)
                pool.drain()
                weights_lo(8, UNITS)
                gathers(L, 0, True)
                with pool.Fori(1, PH) as h:
                    gathers(L, h, False)

        @block.tensor
        def _(pe):
            wq_h, wq_l = (t[:, 0:2, :].rearrange("p a b -> p (a b)") for t in (w_hi, w_lo))

            def product(out, a, b, start, stop):
                nc.tensor.matmul(out, a[0], b[0], start=start, stop=False)
                nc.tensor.matmul(out, a[0], b[1], start=False, stop=False)
                return nc.tensor.matmul(out, a[1], b[0], start=False, stop=stop)

            def transposes(xn_at, full):
                for tt in range(TT):
                    pe.wait_ge(xn_ready.sem, xn_at(tt + 1))
                    for half in range(2):
                        for i in range(4):
                            c = (4 * half + i) * P
                            t = nc.tensor.transpose(M[2 * tt + half][:, i * P:(i + 1) * P], xn[:, tt, c:c + P], ident)
                        t.then_inc(full.sem, 1)

            pe.wait_ge(const_in.sem, 16)
            transposes(lambda k: k, xT_full)

            def peer_scores(L, h):
                pe.wait_ge(wq_lo.sem, wq_lo.at(L, h + 1))
                for half in range(2):
                    for kt in range(KT):
                        q = slice(kt * SEQ + half * P, kt * SEQ + (half + 1) * P)
                        m = product(PJ[0][:, half * SEQ:(half + 1) * SEQ], (wq_h[:, q], wq_l[:, q]),
                                    (h_hi[:, kt, :], h_lo[:, kt, :]), kt == 0, kt == KT - 1)
                m.then_inc(qh_full.sem, 1)
                pe.wait_ge(qh_ready.sem, qh_ready.at(L, h + 1))
                for tt in range(TT):
                    for half in range(2):
                        r = 2 * tt + half
                        m = nc.tensor.matmul(PJ[1][:, r * NKEYS:(r + 1) * NKEYS], qh[:, half, tt * P:(tt + 1) * P],
                                             pr(("k1", "k2")[half]), start=True, stop=True)
                m.then_inc(sk_full.sem, 1)

            def peer_mix(L, h):
                for tt in range(TT):
                    for k in range(TOPK):
                        n = tt * TOPK + k
                        pe.wait_ge(diag_ready.sem, diag_ready.at(L, h * (TT * TOPK) + (n + 1)))
                        for half in range(2):
                            m = nc.tensor.matmul(M[2 * tt + half][:, :], diag[:, k % 4, :],
                                                 rows[:, k % SLOTS, D + half * HALF:D + (half + 1) * HALF],
                                                 start=(k == 0), stop=(k == TOPK - 1))
                        m.then_inc(row_used.sem, 1)

            with pe.Fori(0, depth) as L:
                def unit(n):
                    pe.wait_ge(lo_ready.sem, lo_ready.at(L, n + 1))
                    return w_hi[:, n % RING, :], w_lo[:, n % RING, :]

                def job(j):
                    if j >= 2:
                        pe.wait_ge(proj_free[j % 2].sem, proj_free[j % 2].at(L, j // 2))
                    return PJ[j % 2]

                def both(t, *at):
                    return tuple(v[at] for v in t)

                hT, bT = (h_hi, h_lo), (b_hi, b_lo)
                ALLP = slice(None)

                def tile_T(out, w, i, kts, src, k0=0):
                    for kt in range(kts):
                        q = (i * kts + kt) * P
                        m = product(out, both(w, ALLP, slice(q, q + P)), both(src, ALLP, k0 + kt, ALLP),
                                    kt == 0, kt == kts - 1)
                    return m

                def columns_T(j, n, src):
                    out = job(j)
                    for i in range(2):
                        tile_T(out[:, i * SEQ:(i + 1) * SEQ], unit(n + i), 0, KT, src).then_inc(unit_used.sem, 1)

                def narrow_T(j, n, k0):
                    out, w = job(j), unit(n)
                    for i in range(2):
                        m = tile_T(out[:, i * SEQ:(i + 1) * SEQ], w, i, 4, bT, k0)
                    m.then_inc(unit_used.sem, 1)

                def rows_N(banks, n, units, kts, cols, src):
                    for v in range(units):
                        w = unit(n + v)
                        for tt in range(TT):
                            for k in range(kts):
                                m = product(banks[tt], both(src, ALLP, kts * v + k, slice(tt * P, (tt + 1) * P)),
                                            both(w, ALLP, slice(k * cols, (k + 1) * cols)),
                                            v == 0 and k == 0, v == units - 1 and k == kts - 1)
                        m.then_inc(unit_used.sem, 1)

                transposes(lambda k: xn_ready.at(L, k), xT_full)
                pe.wait_ge(hT_ready.sem, hT_ready.at(L, 4))
                for n in range(2):
                    columns_T(J_QKVUX + n, U_QKVUX + 2 * n, hT)
                out = job(J_QKVUX + 2)
                tile_T(out[:, 0:SEQ], unit(U_QKVUX + 4), 0, KT, hT).then_inc(unit_used.sem, 1)
                rows_N([out[:, SEQ + tt * P:SEQ + (tt + 1) * P] for tt in range(TT)], U_QKVUX + 5, 1, KT, P, hT)
                pe.wait_ge(proj_free[0].sem, proj_free[0].at(L, 2))
                pe.wait_ge(proj_free[1].sem, proj_free[1].at(L, 1))
                for G in range(KVH):
                    g = slice(64 * G, 64 * G + 64)
                    for j in range(REP):
                        m = nc.tensor.matmul(M[G][:, j * P:(j + 1) * P], qT[g, j, 0:P], kT[g, 0:P], start=True, stop=True)
                    m.then_inc(score_full.sem, 1)
                for G in range(KVH):
                    g = slice(64 * G, 64 * G + 64)
                    for j in range(REP):
                        m = nc.tensor.matmul(M[2 + 2 * G + j // 2][:, (j % 2) * SEQ:(j % 2 + 1) * SEQ], qT[g, j, P:SEQ],
                                             kT[g, :], start=True, stop=True)
                    m.then_inc(score_full.sem, 1)
                for n in range(3, 5):
                    columns_T(J_QKVUX + n, U_QKVUX + 2 * n, hT)
                pe.wait_ge(frames_ready.sem, frames_ready.at(L, 1))
                pe.wait_ge(score_read.sem, score_read.at(L, 1))
                for part in range(2):
                    for c in range(4):
                        t = nc.tensor.transpose(M[part][:, c * P:(c + 1) * P], Zflat[part][:, c * P:(c + 1) * P], ident)
                    t.then_inc(zT_full.sem, 1)

                def s5_inputs(c):
                    if c == 0:
                        pe.wait_ge(zT_ready.sem, zT_ready.at(L, 2))
                    else:
                        pe.wait_ge(bu_read.sem, bu_read.at(L, c))
                    for part in range(2):
                        for b in range(4):
                            r = slice(32 * b, 32 * b + 32)
                            m = nc.tensor.matmul(M[b][:, part * SEQ:(part + 1) * SEQ], Zflat[part][r, c * P:(c + 1) * P],
                                                 uT[r, c, :], start=True, stop=True)
                    m.then_inc(bu_full.sem, 1)

                def s5_outputs(c):
                    pe.wait_ge(state_ready.sem, state_ready.at(L, c + 1))
                    if c >= 2:
                        pe.wait_ge(ys5_pre.sem, ys5_pre.at(L, c - 1))
                    for part, (mat, val) in enumerate(((Cr, xr_), (Ci, xi_))):
                        for b in range(4):
                            m = nc.tensor.matmul(M[4 + c % 2][32 * b:32 * b + 32, 0:SEQ], mat[:, 4 * c + b, :],
                                                 val[:, b, :], start=(part == 0), stop=(part == 1))
                    m.then_inc(y_full.sem, 1)

                s5_inputs(0)
                columns_T(J_QKVUX + 5, U_QKVUX + 10, hT)
                s5_inputs(1)
                for n in range(6, 8):
                    columns_T(J_QKVUX + n, U_QKVUX + 2 * n, hT)
                s5_outputs(0)
                s5_inputs(2)
                for n in range(8, 10):
                    columns_T(J_QKVUX + n, U_QKVUX + 2 * n, hT)
                s5_outputs(1)
                pe.wait_ge(hm_ready.sem, hm_ready.at(L, 1))
                columns_T(J_XK, U_XK, bT)
                s5_inputs(3)
                out, halves = job(J_XV), (unit(U_XV), unit(U_XV + 1))
                for tt in range(TT):
                    for kt in range(KT):
                        k = (kt % 4) * SEQ
                        m = product(out[:, tt * SEQ:(tt + 1) * SEQ], both(bT, ALLP, kt, slice(tt * P, (tt + 1) * P)),
                                    both(halves[kt // 4], ALLP, slice(k, k + SEQ)), kt == 0, kt == KT - 1)
                        if tt == TT - 1 and kt % 4 == 3:
                            m.then_inc(unit_used.sem, 1)
                s5_outputs(2)
                rows_N([job(J_Z), job(J_Z + 1)], U_Z, 4, 2, HALF, hT)
                s5_outputs(3)
                rows_N([job(J_Z + 2), job(J_Z + 3)], U_Z + 4, 4, 2, HALF, hT)
                pe.wait_ge(p_ready.sem, p_ready.at(L, 1))
                for G in range(KVH):
                    for j in range(REP):
                        t = nc.tensor.transpose(M[2 + G][:, j * P:(j + 1) * P], sc0[:, 4 * G + j, :], ident)
                    t.then_inc(pT_full.sem, 1)
                pe.wait_ge(ys5_pre.sem, ys5_pre.at(L, 4))
                pe.wait_ge(wdt_ready.sem, wdt_ready.at(L, 1))
                for tt in range(TT):
                    for kt in range(KT):
                        m = product(M[5][:, tt * 16:(tt + 1) * 16], both(hT, ALLP, kt, slice(tt * P, (tt + 1) * P)),
                                    (wdt_hi[:, kt * 16:(kt + 1) * 16], wdt_lo[:, kt * 16:(kt + 1) * 16]),
                                    kt == 0, kt == KT - 1)
                m.then_inc(dt_full.sem, 1)
                pe.wait_ge(pT_ready.sem, pT_ready.at(L, 2))
                for G in range(KVH):
                    m = nc.tensor.matmul(M[4][64 * G:64 * G + 64, :], vN[:, 0, 64 * G:64 * G + 64],
                                         pT0[:, G * HALF:(G + 1) * HALF], start=True, stop=True)
                m.then_inc(o_full.sem, 1)
                pe.wait_ge(p_ready.sem, p_ready.at(L, 2))
                for kb in range(TT):
                    for G in range(KVH):
                        for j in range(REP):
                            t = nc.tensor.transpose(M[2 * kb + G][:, j * P:(j + 1) * P],
                                                    sc1[:, 4 * G + j, kb * P:(kb + 1) * P], ident)
                        t.then_inc(pT_full.sem, 1)
                pe.wait_ge(pT_ready.sem, pT_ready.at(L, 6))
                pe.wait_ge(oT_ready.sem, oT_ready.at(L, 1))
                for G in range(KVH):
                    for kb in range(TT):
                        m = nc.tensor.matmul(M[4][64 * G:64 * G + 64, :], vN[:, kb, 64 * G:64 * G + 64],
                                             pT1[:, kb, G * HALF:(G + 1) * HALF], start=(kb == 0), stop=(kb == 1))
                m.then_inc(o_full.sem, 1)
                for n in range(2):
                    columns_T(J_GAB + n, U_GAB + 2 * n, hT)
                pe.wait_ge(silu_ready.sem, silu_ready.at(L, 2))
                for c in range(2):
                    for half in range(2):
                        for i in range(4):
                            t = nc.tensor.transpose(M[2 * c + half][:, i * P:(i + 1) * P],
                                                    xbcC[:, 4 * half + i, c * P:(c + 1) * P], ident)
                        t.then_inc(xs_full.sem, 1)
                pe.wait_ge(oT_ready.sem, oT_ready.at(L, 2))
                pe.wait_ge(ad_ready.sem, ad_ready.at(L, 1))
                nc.tensor.transpose(M[4][:, 0:P], xbcC[:, 8, 0:P], ident)
                nc.tensor.matmul(M[4][:, 256:272], later, ad[:, 0, :], start=True, stop=True)
                nc.tensor.matmul(M[4][:, 272:288], upto, ad[:, 1, :], start=True, stop=True).then_inc(misc_full.sem, 1)
                for g in range(2):
                    pe.drain()
                    for c in range(2):
                        r = slice(64 * g, 64 * g + 64)
                        q = 2 * c + g
                        m = nc.tensor.matmul(M[5][:, q * P:(q + 1) * P], xbcC[r, 8, c * P:(c + 1) * P],
                                             xbcC[r, 9, c * P:(c + 1) * P], start=True, stop=True)
                m.then_inc(cb_full.sem, 1)
                for n in range(2, 4):
                    columns_T(J_GAB + n, U_GAB + 2 * n, hT)

                def ssd_decays(c):
                    pe.wait_ge(adU_ready.sem, adU_ready.at(L, c + 1))
                    if c == 0:
                        pe.wait_ge(xs_ready.sem, xs_ready.at(L, 4))
                    else:
                        pe.wait_ge(s0_ready.sem, s0_ready.at(L, 1))
                    for q in range(4):
                        nc.tensor.matmul(M[q][:, :], later, adU[:, 4 * q:4 * q + 4, :], start=True, stop=True).then_inc(
                            diff_full.sem, 1)

                def ssd_diagonal(c):
                    pe.wait_ge(w_ready.sem, w_ready.at(L, c + 1))
                    if c == 0:
                        pe.wait_ge(misc_ready.sem, misc_ready.at(L, 1))
                    else:
                        pe.wait_ge(yd_read.sem, yd_read.at(L, 1))
                    for h in range(SSDH):
                        m = nc.tensor.matmul(M[4 + h // 8][:, (h % 8) * HD:(h % 8 + 1) * HD], decayE[:, h, :],
                                             xdt[:, c, h * HD:(h + 1) * HD], start=True, stop=True)
                    m.then_inc(yd_full.sem, 1)

                ssd_decays(0)
                for n in range(4, 8):
                    columns_T(J_GAB + n, U_GAB + 2 * n, hT)
                ssd_diagonal(0)
                pe.wait_ge(xdec_ready.sem, xdec_ready.at(L, 1))
                for g in range(2):
                    m = nc.tensor.matmul(M[0][64 * g:64 * g + 64, :], bN[:, 64 * g:64 * g + 64],
                                         xdec[:, g * HALF:(g + 1) * HALF], start=True, stop=True)
                m.then_inc(s0_full.sem, 1)
                for i in range(2):
                    narrow_T(J_ATTN + i, U_ATTN + i, 0)
                ssd_decays(1)
                for i in range(2, 4):
                    narrow_T(J_ATTN + i, U_ATTN + i, 0)
                for n in range(4):
                    columns_T(J_GC + n, U_GC + 2 * n, hT)
                ssd_diagonal(1)
                pe.wait_ge(decay_ready.sem, decay_ready.at(L, 8))
                for g in range(2):
                    m = nc.tensor.matmul(M[g][:, :], xbcC[64 * g:64 * g + 64, 9, P:SEQ], s0[64 * g:64 * g + 64, :],
                                         start=True, stop=True)
                m.then_inc(yo_full.sem, 1)
                pe.wait_ge(ys5_ready.sem, ys5_ready.at(L, 1))
                for i in range(4):
                    narrow_T(J_GLU + i, U_GLU + i, 4)
                transposes(lambda k: xn_ready.at(L, 2 + k), xT_full)
                for i in range(4, 8):
                    narrow_T(J_GLU + i, U_GLU + i, 4)
                pe.wait_ge(hT_ready.sem, hT_ready.at(L, 8))
                for i in range(4):
                    columns_T(J_SSD + i, U_SSD + 2 * i, hT)
                pe.wait_ge(merged_ready.sem, merged_ready.at(L, 1))
                for c in range(2):
                    rows_N([job(J_WO + 2 * c), job(J_WO + 2 * c + 1)], U_WO + 4 * c, 4, 2, HALF, bT)
                transposes(lambda k: xn_ready.at(L, 4 + k), xT_full)
                pe.wait_ge(hT_ready.sem, hT_ready.at(L, 12))
                columns_T(J_XQ, U_XQ, hT)
                pe.wait_ge(proj_free[0].sem, proj_free[0].at(L, J_XQ // 2 + 1))
                for tt in range(TT):
                    for h in range(XH):
                        r = slice(64 * (h % 2), 64 * (h % 2) + 64)
                        m = nc.tensor.matmul(M[2 * tt + h % 2][:, (h // 2) * SEQ:(h // 2 + 1) * SEQ],
                                             qxT[r, h // 2, tt * P:(tt + 1) * P], kxT[r, h // 2, :], start=True, stop=True)
                    m.then_inc(sx_full.sem, 1)
                for tt in range(TT):
                    pe.wait_ge(px_ready.sem, px_ready.at(L, tt + 1))
                    for kb in range(TT):
                        for h in range(XH):
                            t = nc.tensor.transpose(M[(4, 0)[tt] + kb][:, h * P:(h + 1) * P],
                                                    scx[:, tt, h, kb * P:(kb + 1) * P], ident)
                        t.then_inc(pTx_full.sem, 1)

                def at_bank(h):
                    return 2 * (h % 2) + h // 2

                for tt in range(TT):
                    pe.wait_ge(pTx_ready.sem, pTx_ready.at(L, 2 * tt + 2))
                    for h in range(XH):
                        for kb in range(TT):
                            m = nc.tensor.matmul(
                                M[2 + tt][64 * (h % 2):64 * (h % 2) + 64, (h // 2) * P:(h // 2 + 1) * P],
                                vx[:, kb, h * HD:(h + 1) * HD], pTx[:, tt, :, :].rearrange("p h k -> p (h k)")[
                                    :, kb * HALF + at_bank(h) * P:kb * HALF + (at_bank(h) + 1) * P],
                                start=(kb == 0), stop=(kb == 1))
                    m.then_inc(ox_full.sem, 1)
                pe.wait_ge(ox_ready.sem, ox_ready.at(L, 2))
                for c in range(2):
                    rows_N([job(J_XO + 2 * c), job(J_XO + 2 * c + 1)], U_XO + c, 1, 2, HALF, bT)
                transposes(lambda k: xn_ready.at(L, 6 + k), xT_full)
                pe.wait_ge(hT_ready.sem, hT_ready.at(L, 16))
                peer_scores(L, 0)
                with pe.Fori(0, PH - 1) as h:
                    peer_scores(L, h + 1)
                    peer_mix(L, h)
                peer_mix(L, PH - 1)

        @block.scalar
        def _(act):
            A = nc.scalar.activation

            def norm_root(need, done):
                act.wait_ge(ms_ready.sem, need)
                A(root, ms, ACT.Sqrt).then_inc(root_ready.sem, 1)

            def sin_cos(frac, s, c, hs, sign):
                A(s, frac, ACT.Sin, scale=sign * TWO_PI)
                act.drain()
                A(hs, frac, ACT.Sin, scale=TWO_PI / 2)
                act.drain()
                A(hs, hs, ACT.Square)
                act.drain()
                return A(c, hs, ACT.Copy, scale=-2.0, bias=1.0)

            def s5_angles(need):
                act.wait_ge(s5_arg.sem, need)
                sin_cos(ang, sn16, cs16, hs16, 1.0).then_inc(s5_trig.sem, 1)

            s5_angles(1)
            norm_root(1, 1)

            with act.Fori(0, depth) as L:
                made = [0]

                def weights_hi(upto):
                    for n in range(made[0], min(upto, UNITS)):
                        act.wait_ge(unit_in[n % RING].sem, unit_in[n % RING].at(L, 16 * (n // RING + 1)))
                        if n >= RING:
                            act.wait_ge(unit_used.sem, unit_used.at(L, n - RING + 1))
                        A(w_hi[:, n % RING, :], ring[:, n % RING, :], ACT.Copy).then_inc(hi_ready.sem, 1)
                        made[0] = n + 1

                def evac(j, out, func=ACT.Copy, **kw):
                    weights_hi(UNITS_OF_JOB[j] + 3)
                    act.wait_ge(unit_used.sem, unit_used.at(L, UNITS_OF_JOB[j]))
                    n = out.shape
                    src = PJ[j % 2][:, :] if len(n) == 2 else PJ[j % 2][:, :].rearrange("p (a b) -> p a b", a=n[1])
                    A(out, src, func, **kw).then_inc(proj_free[j % 2].sem, 1)

                act.wait_ge(par_in.sem, par_in.at(L, 16))
                weights_hi(RING)
                norm_root(ms_ready.at(L, 1), 1)
                A(wdt_hi[:, :], pr("wdt"), ACT.Copy).then_inc(wdt_rounded.sem, 1)
                def turns(c):
                    act.drain()
                    for b in range(4):
                        A(phi[:, b, :], cst("time"), ACT.Copy, scale=th2pi[:, 4 * c + b:4 * c + b + 1])
                    act.drain()
                    A(turn, phi, ACT.Copy, bias=MAGIC).then_inc(phi_ready.sem, 1)

                def trig(c):
                    act.wait_ge(frac_ready.sem, frac_ready.at(L, c + 1))
                    if c >= 2:
                        act.wait_ge(state_ready.sem, state_ready.at(L, c - 1))
                    sin_cos(turn, sn[c % 2], cs[c % 2], turn, -1.0).then_inc(trig_ready.sem, 1)

                turns(0)
                trig(0)
                evac(0, qT[:, 0:2, :], scale=HD ** -0.5)
                evac(1, qT[:, 2:4, :], scale=HD ** -0.5)
                weights_hi(UNITS_OF_JOB[2] + 3)
                act.wait_ge(unit_used.sem, unit_used.at(L, UNITS_OF_JOB[2]))
                A(kT, PJ[0][:, 0:SEQ], ACT.Copy)
                A(vN, PJ[0][:, SEQ:2 * SEQ].rearrange("p (a b) -> p a b", a=TT), ACT.Copy).then_inc(
                    proj_free[0].sem, 1)

                turns(1)
                evac(3, uT[:, 0:2, :])
                evac(4, uT[:, 2:4, :])
                for part in range(2):
                    act.wait_ge(zT_full.sem, zT_full.at(L, part + 1))
                    A(Zflat[part], M[part][:, :], ACT.Copy).then_inc(zT_ready.sem, 1)
                trig(1)
                turns(2)
                for tt in range(TT):
                    act.wait_ge(max_ready.sem, max_ready.at(L, tt + 1))
                    s = (sc0, sc1)[tt]
                    for h in range(HEADS):
                        A(s[:, h, :], s[:, h, :], ACT.Exp, bias=nmx[:, tt, h:h + 1], accum_out=sums[:, tt, h:h + 1])
                    A(esink[:, tt, :], sinkd[:, tt, :], ACT.Exp).then_inc(exp_ready.sem, 1)
                    evac(5 + tt, xbcT[:, 2 * tt:2 * tt + 2, 3:3 + SEQ])
                evac(7, xbcT[:, 4:6, 3:3 + SEQ])
                trig(2)
                turns(3)
                evac(8, xbcT[:, 6:8, 3:3 + SEQ])
                evac(9, xbcT[:, 8:10, 3:3 + SEQ])
                trig(3)
                evac(J_XK, kxT)
                evac(J_XV, vx)
                evac(J_Z, zs[:, 0, 0:HALF], ACT.Silu)
                evac(J_Z + 1, zs[:, 1, 0:HALF], ACT.Silu)
                act.wait_ge(ys5_pre.sem, ys5_pre.at(L, 4))
                A(b_hi[:, 4:8, :], uT[:, :, :], ACT.Gelu_apprx_tanh)
                act.drain()
                A(uT[:, :, :], uT[:, :, :], ACT.Gelu_apprx_tanh).then_inc(ys5_gelu.sem, 1)
                evac(J_Z + 2, zs[:, 0, HALF:D], ACT.Silu)
                evac(J_Z + 3, zs[:, 1, HALF:D], ACT.Silu)
                for G in range(2):
                    act.wait_ge(pT_full.sem, pT_full.at(L, G + 1))
                    A(pT0[:, G * HALF:(G + 1) * HALF], M[2 + G][:, :], ACT.Copy).then_inc(pT_ready.sem, 1)
                act.wait_ge(dt_arg.sem, dt_arg.at(L, 1))
                A(sp_e, sp_a, ACT.Exp, scale=-1.0)
                A(nega, pr("alog"), ACT.Exp).then_inc(dt_exp.sem, 1)
                act.wait_ge(dt_one.sem, dt_one.at(L, 1))
                A(sp_l, sp_d, ACT.Ln).then_inc(dt_log.sem, 1)
                for q in range(4):
                    act.wait_ge(pT_full.sem, pT_full.at(L, 3 + q))
                    A(pT1[:, q // 2, (q % 2) * HALF:(q % 2 + 1) * HALF], M[q][:, :], ACT.Copy).then_inc(pT_ready.sem, 1)
                evac(J_GAB, gT[:, 0:2, :], ACT.Sigmoid)
                evac(J_GAB + 1, gT[:, 2:4, :], ACT.Sigmoid)
                for half in range(2):
                    act.wait_ge(conv_ready.sem, conv_ready.at(L, half + 1))
                    A(xbcC[:, 5 * half:5 * half + 5, :], xbcC[:, 5 * half:5 * half + 5, :], ACT.Silu).then_inc(
                        silu_ready.sem, 1)
                for c in range(2):
                    for half in range(2):
                        act.wait_ge(xs_full.sem, xs_full.at(L, 2 * c + half + 1))
                        A(xsn[:, c, half * HALF:(half + 1) * HALF], M[2 * c + half][:, :], ACT.Copy).then_inc(xs_ready.sem, 1)
                act.wait_ge(misc_full.sem, misc_full.at(L, 1))
                A(bN, M[4][:, 0:P], ACT.Copy)
                A(dec0, M[4][:, 256:272], ACT.Exp)
                A(eac1, M[4][:, 272:288], ACT.Exp).then_inc(misc_ready.sem, 1)
                evac(J_GAB + 2, gT[:, 4:6, :], ACT.Sigmoid)
                evac(J_GAB + 3, gT[:, 6:8, :], ACT.Sigmoid)

                def decays(c):
                    for q in range(4):
                        act.wait_ge(diff_full.sem, diff_full.at(L, 4 * c + q + 1))
                        if c == 1 and q == 0:
                            act.wait_ge(yd_full.sem, yd_full.at(L, 1))
                        A(decayE[:, 4 * q:4 * q + 4, :], M[q][:, :].rearrange("p (h l) -> p h l", h=4),
                          ACT.Exp).then_inc(decay_ready.sem, 1)

                decays(0)
                for n in range(4, 8):
                    evac(J_GAB + n, gT[:, 2 * n:2 * n + 2, :], ACT.Sigmoid)
                act.wait_ge(s0_full.sem, s0_full.at(L, 1))
                A(s0, M[0][:, :], ACT.Copy).then_inc(s0_ready.sem, 1)
                weights_hi(UNITS_OF_JOB[J_ATTN + 1] + 3)
                decays(1)
                for n in range(4):
                    freed = proj_free[(J_ATTN + n) % 2]
                    act.wait_ge(freed.sem, freed.at(L, (J_ATTN + n) // 2 + 1))
                    evac(J_GC + n, gT[:, 2 * n:2 * n + 2, :], ACT.Sigmoid)
                for i in range(4):
                    if i >= 2:
                        act.wait_ge(sg_used.sem, sg_used.at(L, i - 1))
                    evac(J_GLU + 2 * i, sgate[:, i % 2, :], ACT.Sigmoid)
                    if i == 0:
                        norm_root(ms_ready.at(L, 2), 1)
                weights_hi(U_WO + 3)
                act.wait_ge(merged_ready.sem, merged_ready.at(L, 1))
                weights_hi(U_XQ + 3)
                norm_root(ms_ready.at(L, 3), 1)
                evac(J_XQ, qxT)
                for tt in range(TT):
                    act.wait_ge(mxx_ready.sem, mxx_ready.at(L, tt + 1))
                    for h in range(XH):
                        A(scx[:, tt, h, :], M[2 * tt + h // 2][:, (h % 2) * SEQ:(h % 2 + 1) * SEQ], ACT.Exp,
                          scale=HD ** -0.5, bias=mxx[:, tt, h:h + 1], accum_out=sumx[:, tt, h:h + 1])
                    A(small[:, 799:800], small[:, 799:800], ACT.Copy).then_inc(expx_ready.sem, 1)
                    act.drain()
                for tt in range(TT):
                    for kb in range(TT):
                        act.wait_ge(pTx_full.sem, pTx_full.at(L, 2 * tt + kb + 1))
                        A(pTx[:, tt, :, :].rearrange("p h k -> p (h k)")[:, kb * HALF:(kb + 1) * HALF],
                          M[(4, 0)[tt] + kb][:, :], ACT.Copy).then_inc(pTx_ready.sem, 1)
                assert made[0] == UNITS

                def peer_hi(h):
                    act.wait_ge(wq_in.sem, wq_in.at(L, h * 16 + 16))
                    A(w_hi[:, 0:2, :], wq, ACT.Copy).then_inc(wq_hi.sem, 1)

                def peer_out(h):
                    act.wait_ge(qh_full.sem, qh_full.at(L, h + 1))
                    A(qh, PJ[0][:, :].rearrange("p (a t) -> p a t", a=2), ACT.Copy).then_inc(qh_ready.sem, 1)
                    act.wait_ge(sk_full.sem, sk_full.at(L, h + 1))
                    A(sk, PJ[1][:, :].rearrange("p (r k) -> p r k", r=4), ACT.Copy).then_inc(sk_ready.sem, 1)

                def peer_exp(h, tt):
                    act.wait_ge(top_ready.sem, top_ready.at(L, h * TT + (tt + 1)))
                    A(gnext[:, tt, :], gnext[:, tt, :], ACT.Exp, accum_out=psum16[:, tt:tt + 1])
                    A(small[:, 799:800], small[:, 799:800], ACT.Copy).then_inc(topexp_ready.sem, 1)
                    act.drain()

                def peer_weights(h, tt, more, convert):
                    for k in range(TOPK):
                        n = tt * TOPK + k
                        act.wait_ge(dot_ready.sem, dot_ready.at(L, h * (TT * TOPK) + (n + 1)))
                        A(act_gelu[:, k:k + 1], act_dot[:, k:k + 1], ACT.Gelu_apprx_tanh)
                        act.drain()
                        A(act_w[:, k:k + 1], act_gelu[:, k:k + 1], ACT.Copy, scale=gcur[:, tt, k:k + 1])
                        act.drain()
                        if n >= 4:
                            act.wait_ge(row_used.sem, row_used.at(L, h * (TT * TOPK) + (n - 3)))
                        A(diag[:, k % 4, :], ident, ACT.Copy, scale=act_w[:, k:k + 1]).then_inc(diag_ready.sem, 1)
                        if k == 12 and more:
                            peer_exp(h + 1, tt)
                        if k == 10 and convert and tt == 0:
                            peer_hi(h + 2)
                    if not more and tt == 0:
                        s5_angles(s5_arg.at(L, 1))

                def peer_of(h, convert):
                    peer_out(h + 1)
                    for tt in range(TT):
                        peer_weights(h, tt, True, convert)
                    act.wait_ge(row_used.sem, row_used.at(L, (h + 1) * (TT * TOPK)))
                    A(small[:, 798:799], small[:, 798:799], ACT.Copy)

                act.wait_ge(unit_used.sem, unit_used.at(L, U_XO))
                peer_hi(0)
                norm_root(ms_ready.at(L, 4), 1)
                peer_out(0)
                peer_exp(0, 0)
                peer_exp(0, 1)
                peer_hi(1)
                with act.Fori(0, PH - 2) as h:
                    peer_of(h, True)
                peer_of(PH - 2, False)
                for tt in range(TT):
                    peer_weights(PH - 1, tt, False, False)
                act.drain()
            norm_root(ms_ready.at(depth, 1), 1)

        @block.vector
        def _(dve):
            V = nc.vector
            TS, TTn, STT = V.tensor_scalar, V.tensor_tensor, V.scalar_tensor_tensor

            def bc(ap, axis, shape):
                return ap.unsqueeze(axis).to_broadcast(shape)

            def norm_sums(src):
                for tt in range(TT):
                    V.tensor_tensor_reduce(out=xn[:, tt, :], in0=src[:, tt, :], in1=src[:, tt, :], scale=1.0, scalar=0.0,
                                           op0=ALU.mult, op1=ALU.add, accum_out=ssq[:, tt:tt + 1])
                dve.drain()
                TS(ms, ssq, 1.0 / D, EPS, ALU.mult, ALU.add).then_inc(ms_ready.sem, 1)

            def norm_rows(src, root_at, gain=None):
                dve.wait_ge(root_ready.sem, root_at)
                V.reciprocal(rstd, root)
                dve.drain()
                for tt in range(TT):
                    if gain is None:
                        TS(xn[:, tt, :], src[:, tt, :], rstd[:, tt:tt + 1], None, ALU.mult).then_inc(xn_ready.sem, 1)
                    else:
                        i = STT(xn[:, tt, :], src[:, tt, :], rstd[:, tt:tt + 1], gain, ALU.mult, ALU.mult)
                        i.then_inc(xn_ready.sem, 1)

            def norm(src, root_at, gain=None):
                norm_sums(src)
                norm_rows(src, root_at, gain)

            def cut_in_two(hi, lo, v):
                V.tensor_copy(hi, v)
                dve.drain()
                return TTn(lo, v, hi.bitcast(F32), ALU.subtract)

            def norm_T(full_at, gain, tiles=range(TT)):
                for tt in tiles:
                    for half in range(2):
                        dve.wait_ge(xT_full.sem, full_at(2 * tt + half + 1))
                        ks, ts = slice(4 * half, 4 * half + 4), slice(tt * P, (tt + 1) * P)
                        src = M[2 * tt + half][:, :].rearrange("p (i t) -> p i t", i=4)
                        if gain is None:
                            i = cut_in_two(h_hi[:, ks, ts], h_lo[:, ks, ts], src)
                        else:
                            TTn(h_hi[:, ks, ts], src, bc(gain[:, ks], 2, [P, 4, P]), ALU.mult)
                            dve.drain()
                            for k in range(4):
                                kt = 4 * half + k
                                i = STT(h_lo[:, kt, ts], src[:, k, :], gain[:, kt:kt + 1],
                                        h_hi[:, kt, ts].bitcast(F32), ALU.mult, ALU.subtract)
                        i.then_inc(hT_ready.sem, 1)

            def exp_exact(out, z):
                TS(e_n, z, 1.4426950408889634, MAGIC, ALU.mult, ALU.add)
                dve.drain()
                TS(e_n, e_n, MAGIC, -126.0, ALU.subtract, ALU.max)
                dve.drain()
                TS(e_n, e_n, 127.0, None, ALU.min)
                dve.drain()
                STT(e_f, e_n, -0.693359375, z, ALU.mult, ALU.add)
                dve.drain()
                STT(e_f, e_n, 2.12194440e-4, e_f, ALU.mult, ALU.add)
                TS(e_i[:, :], e_n, 127.0, 8388608.0, ALU.add, ALU.mult)
                dve.drain()
                TS(e_p, e_f, 1.0 / 5040, None, ALU.mult)
                for c in (1 / 720, 1 / 120, 1 / 24, 1 / 6, 0.5, 1.0):
                    dve.drain()
                    STT(e_p, e_p, c, e_f, ALU.add, ALU.mult)
                dve.drain()
                STT(out, e_p, 1.0, e_i[:, :].bitcast(F32), ALU.add, ALU.mult)
                dve.drain()

            def s5_small():
                exp_exact(dts5, pr("ldt"))
                TTn(la, pr("lr"), dts5, ALU.mult)
                TTn(th, pr("li"), dts5, ALU.mult)
                dve.drain()
                TS(th2pi, th, 1.0 / (2 * math.pi), None, ALU.mult)
                dve.drain()
                TS(t16a, th2pi, MAGIC, MAGIC, ALU.add, ALU.subtract)
                dve.drain()
                TTn(ang, th2pi, t16a, ALU.subtract).then_inc(s5_arg.sem, 1)
                exp_exact(mag, la)

            V.memset(layer_base, 0.0)
            V.memset(small[:, 798:800], 0.0)
            dve.wait_ge(par_in.sem, 16)
            s5_small()
            dve.wait_ge(mem_in.sem, 16)
            norm(memN, 1)
            for tt in range(TT):
                for half in range(2):
                    dve.wait_ge(xT_full.sem, 2 * tt + half + 1)
                    V.tensor_copy(memT0[:, 4 * half:4 * half + 4, tt * P:(tt + 1) * P], M[2 * tt + half][:, :].rearrange(
                        "p (i t) -> p i t", i=4)).then_inc(hT_ready.sem, 1)
            dve.drain()
            V.tensor_copy(eid[:, 3:4], layer_base).then_inc(memT_made.sem, 1)
            dve.wait_ge(const_in.sem, 16)
            dve.wait_ge(x_in.sem, 16)

            def routing_halves(h, tt):
                for half in range(2):
                    r = 2 * tt + half
                    V.max(topv[:, r, 0:8], sk[:, r, :])
                dve.drain()
                for half in range(2):
                    r = 2 * tt + half
                    V.max_index(topi[:, r, 0:8], topv[:, r, 0:8], sk[:, r, :])
                    V.match_replace(skw[:, r, :], topv[:, r, 0:8], sk[:, r, :], -3e38)
                dve.drain()
                for half in range(2):
                    r = 2 * tt + half
                    V.max(topv[:, r, 8:16], skw[:, r, :])
                dve.drain()
                for half in range(2):
                    r = 2 * tt + half
                    V.max_index(topi[:, r, 8:16], topv[:, r, 8:16], skw[:, r, :])
                dve.drain()

            def routing_pairs(h, tt):
                a, b = 2 * tt, 2 * tt + 1
                c = cand[:, tt, :].rearrange("p (i j) -> p i j", i=16)
                TTn(c, bc(topv[:, a, :], 2, [P, 16, 16]), bc(topv[:, b, :], 1, [P, 16, 16]), ALU.add)
                V.tensor_copy(topf[:, a:b + 1, :], topi[:, a:b + 1, :])
                dve.drain()
                V.max(ctop[:, tt, 0:8], cand[:, tt, :])
                dve.drain()
                V.max_index(cpos[:, tt, 0:8], ctop[:, tt, 0:8], cand[:, tt, :])
                V.match_replace(candw[:, tt, :], ctop[:, tt, 0:8], cand[:, tt, :], -3e38)
                dve.drain()
                V.max(ctop[:, tt, 8:16], candw[:, tt, :])
                dve.drain()
                V.max_index(cpos[:, tt, 8:16], ctop[:, tt, 8:16], candw[:, tt, :])
                TS(gnext[:, tt, :], ctop[:, tt, :], ctop[:, tt, 0:1], None, ALU.subtract).then_inc(top_ready.sem, 1)
                dve.drain()

            def routing_experts(h, tt):
                TS(cab[:, 0, :], cpos[:, tt, :], 4, None, ALU.logical_shift_right)
                TS(cab[:, 1, :], cpos[:, tt, :], 15, None, ALU.bitwise_and)
                dve.drain()
                V.tensor_copy(cabf[:, :, :], cab[:, :, :])
                dve.drain()
                for w in range(2):
                    o = onehot[:, w, :].rearrange("p (k i) -> p k i", k=16)
                    TTn(o, bc(cabf[:, w, :], 2, [P, 16, 16]), bc(cst("iota"), 1, [P, 16, 16]), ALU.is_equal)
                dve.drain()
                for w in range(2):
                    o = onehot[:, w, :].rearrange("p (k i) -> p k i", k=16)
                    TTn(picked[:, w, :].rearrange("p (k i) -> p k i", k=16), o,
                        bc(topf[:, 2 * tt + w, :], 1, [P, 16, 16]), ALU.mult)
                dve.drain()
                V.tensor_reduce(eab[:, :, :], picked.rearrange("p w (k i) -> p w k i", k=16), AX.X, ALU.add)
                dve.drain()
                STT(eid[:, :], eab[:, 0, :], float(NKEYS), eab[:, 1, :], ALU.mult, ALU.add)
                dve.drain()
                TS(idx_next[:, tt, :], eid[:, :], layer_base, None, ALU.add)
                dve.drain()

            def publish(L, h, tt):
                dve.wait_ge(topexp_ready.sem, topexp_ready.at(L, h * TT + (tt + 1)))
                V.reciprocal(psum16[:, tt:tt + 1], psum16[:, tt:tt + 1])
                dve.drain()
                TS(gcur[:, tt, :], gnext[:, tt, :], psum16[:, tt:tt + 1], None, ALU.mult)
                V.tensor_copy(idx[:, tt, :], idx_next[:, tt, :]).then_inc(idx_ready.sem, 1)
                dve.drain()

            def query_rest(L, h):
                dve.wait_ge(wq_hi.sem, wq_hi.at(L, h + 1))
                TTn(w_lo[:, 0:TT, :], wq, w_hi[:, 0:TT, :].bitcast(F32), ALU.subtract).then_inc(wq_lo.sem, 1)

            def peer_head(L, h, more, convert):
                for tt in range(TT):
                    for k in range(TOPK):
                        n = tt * TOPK + k
                        s = k % SLOTS
                        dve.wait_ge(row_in[s].sem, row_in[s].at(L, h * (16 * TT * TOPK // SLOTS) + 16 * (n // SLOTS + 1)))
                        V.tensor_tensor_reduce(out=junk, in0=rows[:, s, 0:D], in1=xn[:, tt, :], scale=1.0, scalar=0.0,
                                               op0=ALU.mult, op1=ALU.add, accum_out=act_dot[:, k:k + 1]).then_inc(
                                                   dot_ready.sem, 1)
                        dve.drain()
                        if more and k == 3:
                            if tt == 0:
                                dve.wait_ge(sk_ready.sem, sk_ready.at(L, h + 2))
                                V.tensor_copy(eid[:, 0:1], layer_base)
                            routing_halves(h + 1, tt)
                        if more and k == 7:
                            routing_pairs(h + 1, tt)
                        if more and k == 11:
                            routing_experts(h + 1, tt)
                        if convert and tt == 0 and k == 13:
                            query_rest(L, h + 2)
                        if not more and tt == 0 and k == 3:
                            dve.wait_ge(par_in.sem, par_in.at(L, 32))
                            s5_small()
                    for half in range(2):
                        c = slice(half * HALF, (half + 1) * HALF)
                        dve.wait_ge(row_used.sem, row_used.at(L, h * (TT * TOPK) + (tt + 1) * TOPK))
                        i = TTn(x[:, tt, c], x[:, tt, c], M[2 * tt + half][:, :], ALU.add)
                    i.then_inc(peer_added.sem, 1)
                    if more:
                        publish(L, h + 1, tt)

            with dve.Fori(0, depth) as L:
                dve.drain()
                norm(x, root_ready.at(L, 1))
                norm_T(lambda k: xT_full.at(L, k), pr("g_mix"))
                def fractions(c):
                    dve.wait_ge(phi_ready.sem, phi_ready.at(L, c + 1))
                    STT(turn, turn, MAGIC, phi, ALU.subtract, ALU.subtract).then_inc(frac_ready.sem, 1)

                fractions(0)
                TTn(t16a, pr("lr"), pr("lr"), ALU.mult)
                TTn(t16b, pr("li"), pr("li"), ALU.mult)
                dve.drain()
                TTn(den, t16a, t16b, ALU.add)
                dve.drain()
                V.reciprocal(den, den)
                dve.wait_ge(s5_trig.sem, s5_trig.at(L, 0))
                TTn(ar, mag, cs16, ALU.mult)
                TTn(ai, mag, sn16, ALU.mult)
                dve.drain()
                TS(nr, ar, -1.0, None, ALU.add)
                dve.drain()
                TTn(wr, nr, pr("lr"), ALU.mult)
                TTn(t16a, ai, pr("li"), ALU.mult)
                TTn(wi, ai, pr("lr"), ALU.mult)
                TTn(t16b, nr, pr("li"), ALU.mult)
                dve.drain()
                TTn(wr, wr, t16a, ALU.add)
                TTn(wi, wi, t16b, ALU.subtract)
                dve.drain()
                TTn(wr, wr, den, ALU.mult)
                TTn(wi, wi, den, ALU.mult)
                dve.drain()

                def b3(ap):
                    return ap.rearrange("p (j i) -> p j i", i=16)
                wr3, wi3 = bc(wr, 2, [P, 16, 16]), bc(wi, 2, [P, 16, 16])
                bre, bim = b3(pr("bre")), b3(pr("bim"))
                TTn(b3(bb[:, 0, :]), bre, wr3, ALU.mult)
                TTn(b3(bb[:, 2, :]), bim, wi3, ALU.mult)
                TTn(b3(bb[:, 1, :]), bim, wr3, ALU.mult)
                dve.drain()
                TTn(bb[:, 0, :], bb[:, 0, :], bb[:, 2, :], ALU.subtract)
                dve.drain()
                TTn(b3(bb[:, 2, :]), bre, wi3, ALU.mult)
                dve.drain()
                TTn(bb[:, 1, :], bb[:, 1, :], bb[:, 2, :], ALU.add).then_inc(bb_ready.sem, 1)
                dve.wait_ge(wdt_rounded.sem, wdt_rounded.at(L, 1))
                TTn(wdt_lo[:, :], pr("wdt"), wdt_hi[:, :].bitcast(F32), ALU.subtract).then_inc(wdt_ready.sem, 1)

                for G in range(KVH):
                    dve.wait_ge(score_full.sem, score_full.at(L, G + 1))
                    for h in range(REP * G, REP * G + REP):
                        STT(sc0[:, h, :], cst("dist")[:, P:2 * P], -2.0 ** (-8 * (h + 1) / HEADS),
                            M[G][:, (h % REP) * P:(h % REP + 1) * P], ALU.mult, ALU.add)
                for G in range(KVH):
                    dve.wait_ge(score_full.sem, score_full.at(L, 3 + G))
                    for h in range(REP * G, REP * G + REP):
                        i = STT(sc1[:, h, :], cst("dist"), -2.0 ** (-8 * (h + 1) / HEADS),
                                M[2 + h // 2][:, (h % 2) * SEQ:(h % 2 + 1) * SEQ], ALU.mult, ALU.add)
                i.then_inc(score_read.sem, 1)
                dve.drain()
                for tt in range(TT):
                    V.tensor_reduce(mx[:, tt, :], (sc0, sc1)[tt], AX.X, ALU.max)
                dve.drain()
                for tt in range(TT):
                    TTn(mx[:, tt, :], mx[:, tt, :], pr("sinks"), ALU.max)
                dve.drain()
                for tt in range(TT):
                    TTn(sinkd[:, tt, :], pr("sinks"), mx[:, tt, :], ALU.subtract)
                    TS(nmx[:, tt, :], mx[:, tt, :], -1.0, None, ALU.mult).then_inc(max_ready.sem, 1)
                fractions(1)
                dve.wait_ge(memT_in.sem, memT_in.at(L, 16))
                TTn(memT, memT, bc(pr("g_mem"), 2, [P, KT, SEQ]), ALU.mult)
                dve.drain()
                cut_in_two(b_hi[:, :, :], b_lo[:, :, :], memT).then_inc(hm_ready.sem, 1)
                dve.drain()

                def s5_out(c):
                    dve.wait_ge(y_full.sem, y_full.at(L, c + 1))
                    STT(uT[:, c, :], uT[:, c, :], pr("s5d")[:, c:c + 1], M[4 + c % 2][:, 0:SEQ], ALU.mult, ALU.add).then_inc(
                        ys5_pre.sem, 1)

                for c in range(4):
                    br, bi, S, C = psum[:, 2:6, 0:SEQ], psum[:, 2:6, SEQ:2 * SEQ], sn[c % 2], cs[c % 2]
                    dve.wait_ge(trig_ready.sem, trig_ready.at(L, c + 1))
                    dve.wait_ge(bu_full.sem, bu_full.at(L, c + 1))
                    TTn(rot_r, br, C, ALU.mult)
                    TTn(tmp1, br, S, ALU.mult)
                    TTn(tmp2, bi, S, ALU.mult)
                    TTn(rot_i, bi, C, ALU.mult).then_inc(bu_read.sem, 1)
                    dve.drain()
                    TTn(rot_r, rot_r, tmp2, ALU.add)
                    TTn(rot_i, rot_i, tmp1, ALU.subtract)
                    dve.drain()
                    for v in (rot_r, rot_i):
                        for b in range(4):
                            V.tensor_tensor_scan(v[:, b, :], mag[:, 4 * c + b:4 * c + b + 1].to_broadcast([P, SEQ]),
                                                 v[:, b, :], 0.0, ALU.mult, ALU.add)
                    if c < 2:
                        fractions(c + 2)
                    if c >= 1:
                        s5_out(c - 1)
                    dve.drain()
                    TTn(xr_, rot_r, C, ALU.mult)
                    TTn(tmp1, rot_i, S, ALU.mult)
                    TTn(xi_, rot_r, S, ALU.mult)
                    TTn(tmp2, rot_i, C, ALU.mult)
                    dve.drain()
                    TTn(xr_, xr_, tmp1, ALU.subtract)
                    TTn(xi_, xi_, tmp2, ALU.add).then_inc(state_ready.sem, 1)
                    if c == 0:
                        for tt in range(TT):
                            dve.wait_ge(exp_ready.sem, exp_ready.at(L, tt + 1))
                            TTn(sums[:, tt, :], sums[:, tt, :], esink[:, tt, :], ALU.add)
                            dve.drain()
                            V.reciprocal(sums[:, tt, :], sums[:, tt, :])
                            dve.drain()
                            s = (sc0, sc1)[tt]
                            TTn(s, s, bc(sums[:, tt, :], 2, [P, HEADS, P * (tt + 1)]), ALU.mult).then_inc(p_ready.sem, 1)
                    dve.drain()

                V.memset(xbcT[:, :, 0:3], 0.0)
                cw = pr("convw").rearrange("p (c k) -> p c k", k=4)
                dve.wait_ge(proj_free[1].sem, proj_free[1].at(L, 5))
                dve.wait_ge(proj_free[0].sem, proj_free[0].at(L, 5))
                V.tensor_copy(eid[:, 1:2], layer_base)
                dve.drain()
                for k in range(4):
                    for c in range(10):
                        src = xbcT[:, c, k:k + SEQ]
                        if k == 0:
                            TS(xbcC[:, c, :], src, cw[:, c, 0:1], pr("convb")[:, c:c + 1], ALU.mult, ALU.add)
                        else:
                            i = STT(xbcC[:, c, :], src, cw[:, c, k:k + 1], xbcC[:, c, :], ALU.mult, ALU.add)
                            if k == 3 and c in (4, 9):
                                i.then_inc(conv_ready.sem, 1)
                    if k == 0:
                        s5_out(3)
                    dve.drain()

                def attention_out(tt):
                    dve.wait_ge(o_full.sem, o_full.at(L, tt + 1))
                    ts = slice(tt * P, (tt + 1) * P)
                    cut_in_two(b_hi[:, 0:4, ts], b_lo[:, 0:4, ts],
                               M[4][:, :].rearrange("p (j t) -> p j t", j=4)).then_inc(oT_ready.sem, 1)

                dve.wait_ge(ys5_gelu.sem, ys5_gelu.at(L, 1))
                TTn(b_lo[:, 4:8, :], uT[:, :, :], b_hi[:, 4:8, :].bitcast(F32), ALU.subtract).then_inc(ys5_ready.sem, 1)
                dve.wait_ge(dt_full.sem, dt_full.at(L, 1))
                TTn(dts, M[5][:, 0:32].rearrange("p (t h) -> p t h", t=TT), bc(pr("dtb"), 1, [P, TT, 16]), ALU.add)
                dve.drain()
                TS(sp_d, dts, -1.0, None, ALU.mult)
                dve.drain()
                TTn(sp_a, sp_d, dts, ALU.max).then_inc(dt_arg.sem, 1)
                TS(dts, dts, 0.0, None, ALU.max)
                attention_out(0)
                dve.wait_ge(dt_exp.sem, dt_exp.at(L, 1))
                TS(sp_d, sp_e, 1.0, None, ALU.add).then_inc(dt_one.sem, 1)
                dve.drain()
                TS(sp_a, sp_d, -1.0, 1e-30, ALU.add, ALU.add)
                dve.wait_ge(dt_log.sem, dt_log.at(L, 1))
                TS(sp_l, sp_l, 1e-30, None, ALU.add)
                dve.drain()
                V.reciprocal(sp_a, sp_a)
                TTn(sp_l, sp_l, sp_e, ALU.mult)
                dve.drain()
                TTn(sp_l, sp_l, sp_a, ALU.mult)
                dve.drain()
                TTn(dts, dts, sp_l, ALU.add)
                dve.drain()
                STT(ad, dts, -1.0, bc(nega, 1, [P, TT, 16]), ALU.mult, ALU.mult).then_inc(ad_ready.sem, 1)
                attention_out(1)

                def h3(ap):
                    return ap.rearrange("p (h d) -> p h d", h=SSDH)

                dve.wait_ge(cb_full.sem, cb_full.at(L, 1))
                TTn(cbm, M[5][:, :].rearrange("p (q l) -> p q l", q=4), bc(upto, 1, [P, 4, P]), ALU.mult).then_inc(
                    cb_ready.sem, 1)
                dve.drain()
                for c in range(2):
                    if c == 1:
                        dve.wait_ge(diff_full.sem, diff_full.at(L, 4))
                    TTn(adU, bc(ad[:, c, :], 2, [P, SSDH, P]), bc(upto, 1, [P, SSDH, P]), ALU.mult).then_inc(
                        adU_ready.sem, 1)
                    dve.wait_ge(xs_ready.sem, xs_ready.at(L, 2 * c + 2))
                    TTn(h3(xdt[:, c, :]), h3(xsn[:, c, :]), bc(dts[:, c, :], 2, [P, SSDH, HD]), ALU.mult)
                    TTn(h3(ytmp), h3(xsn[:, c, :]), bc(pr("ssdd"), 2, [P, SSDH, HD]), ALU.mult)
                    if c == 0:
                        dve.drain()
                        dve.wait_ge(misc_ready.sem, misc_ready.at(L, 1))
                        TTn(h3(xdec), h3(xdt[:, 0, :]), bc(dec0, 2, [P, SSDH, HD]), ALU.mult).then_inc(xdec_ready.sem, 1)
                    if c == 1:
                        for i in range(4):
                            dve.wait_ge(unit_used.sem, unit_used.at(L, UNITS_OF_JOB[J_ATTN + i]))
                            TTn(mergedT[:, 2 * i:2 * i + 2, :], PJ[(J_ATTN + i) % 2][:, :].rearrange(
                                "p (a t) -> p a t", a=2), gT[:, 2 * i:2 * i + 2, :], ALU.mult).then_inc(
                                    proj_free[(J_ATTN + i) % 2].sem, 1)
                    dve.wait_ge(decay_ready.sem, decay_ready.at(L, 4 * c + 4))
                    for g in range(2):
                        v = decayE[:, 8 * g:8 * g + 8, :]
                        i = TTn(v, v, bc(cbm[:, 2 * c + g, :], 1, [P, 8, P]), ALU.mult)
                    i.then_inc(w_ready.sem, 1)
                    dve.wait_ge(yd_full.sem, yd_full.at(L, c + 1))
                    for half in range(2):
                        q = slice(half * HALF, (half + 1) * HALF)
                        i = TTn(xn[:, c, q], ytmp[:, q], M[4 + half][:, :], ALU.add)
                    i.then_inc(yd_read.sem, 1)
                    dve.drain()
                    if c == 1:
                        dve.wait_ge(yo_full.sem, yo_full.at(L, 1))
                        for g in range(2):
                            q = slice(g * HALF, (g + 1) * HALF)
                            TTn(ytmp[:, q].rearrange("p (h d) -> p h d", h=8), M[g][:, :].rearrange(
                                "p (h d) -> p h d", h=8), bc(eac1[:, 8 * g:8 * g + 8], 2, [P, 8, HD]), ALU.mult)
                        dve.drain()
                        TTn(xn[:, 1, :], xn[:, 1, :], ytmp, ALU.add)
                        dve.drain()
                def s5_branch(i):
                    jb, ja = J_GLU + 2 * i, J_GLU + 2 * i + 1
                    dve.wait_ge(proj_free[jb % 2].sem, proj_free[jb % 2].at(L, jb // 2 + 1))
                    dve.wait_ge(unit_used.sem, unit_used.at(L, UNITS_OF_JOB[ja]))
                    TTn(ytmp[:, 0:HALF], PJ[ja % 2][:, :], sgate[:, i % 2, :], ALU.mult).then_inc(proj_free[ja % 2].sem, 1)
                    dve.drain()
                    yv = ytmp[:, 0:HALF].rearrange("p (a t) -> p a t", a=2)
                    TTn(yv, yv, gT[:, 8 + 2 * i:10 + 2 * i, :], ALU.mult).then_inc(sg_used.sem, 1)
                    dve.drain()
                    m = mergedT[:, 2 * i:2 * i + 2, :]
                    TTn(m, m, yv, ALU.add)
                    dve.drain()

                TTn(zs[:, :, :], xn[:, :, :], zs[:, :, :], ALU.mult)
                dve.drain()
                norm_sums(zs)
                s5_branch(0)
                norm_rows(zs, root_ready.at(L, 2))
                s5_branch(1)
                for tt in range(TT):
                    norm_T(lambda k: xT_full.at(L, 4 + k), pr("g_ssd"), (tt,))
                    s5_branch(2 + tt)
                for i in range(4):
                    dve.wait_ge(unit_used.sem, unit_used.at(L, UNITS_OF_JOB[J_SSD + i]))
                    yv = ytmp[:, 0:HALF].rearrange("p (a t) -> p a t", a=2)
                    TTn(yv, PJ[(J_SSD + i) % 2][:, :].rearrange("p (a t) -> p a t", a=2),
                        gT[:, 2 * i:2 * i + 2, :], ALU.mult).then_inc(proj_free[(J_SSD + i) % 2].sem, 1)
                    dve.drain()
                    m = mergedT[:, 2 * i:2 * i + 2, :]
                    TTn(m, m, yv, ALU.add)
                    dve.drain()
                    last = cut_in_two(b_hi[:, 2 * i:2 * i + 2, :], b_lo[:, 2 * i:2 * i + 2, :], m)
                last.then_inc(merged_ready.sem, 1)

                def add_to_x(j, tt, c):
                    dve.wait_ge(unit_used.sem, unit_used.at(L, UNITS_OF_JOB[j]))
                    q = slice(c * HALF, (c + 1) * HALF)
                    TTn(x[:, tt, q], x[:, tt, q], PJ[j % 2][:, :], ALU.add).then_inc(proj_free[j % 2].sem, 1)

                for c in range(2):
                    for tt in range(TT):
                        add_to_x(J_WO + 2 * c + tt, tt, c)
                dve.drain()
                norm(x, root_ready.at(L, 3))
                norm_T(lambda k: xT_full.at(L, 8 + k), pr("g_x"))
                for tt in range(TT):
                    dve.wait_ge(sx_full.sem, sx_full.at(L, tt + 1))
                    for q in range(2):
                        V.tensor_reduce(sumx[:, tt, 2 * q:2 * q + 2],
                                        M[2 * tt + q][:, :].rearrange("p (a k) -> p a k", a=2), AX.X, ALU.max)
                    dve.drain()
                    TS(mxx[:, tt, :], sumx[:, tt, :], -HD ** -0.5, None, ALU.mult).then_inc(mxx_ready.sem, 1)
                for tt in range(TT):
                    dve.wait_ge(expx_ready.sem, expx_ready.at(L, tt + 1))
                    V.reciprocal(sumx[:, tt, :], sumx[:, tt, :])
                    dve.drain()
                    TTn(scx[:, tt, :, :], scx[:, tt, :, :], bc(sumx[:, tt, :], 2, [P, XH, SEQ]), ALU.mult).then_inc(
                        px_ready.sem, 1)
                for tt in range(TT):
                    dve.wait_ge(ox_full.sem, ox_full.at(L, tt + 1))
                    ts = slice(tt * P, (tt + 1) * P)
                    cut_in_two(b_hi[:, 0:2, ts], b_lo[:, 0:2, ts],
                               M[2 + tt][:, 0:2 * P].rearrange("p (j t) -> p j t", j=2)).then_inc(ox_ready.sem, 1)
                query_rest(L, 0)
                for c in range(2):
                    for tt in range(TT):
                        add_to_x(J_XO + 2 * c + tt, tt, c)
                dve.drain()
                dve.wait_ge(gnat_in.sem, gnat_in.at(L, 16))
                V.tensor_copy(eid[:, 3:4], layer_base)
                norm(x, root_ready.at(L, 4), gain=gnat)
                norm_T(lambda k: xT_full.at(L, 12 + k), None)
                dve.wait_ge(sk_ready.sem, sk_ready.at(L, 1))
                V.tensor_copy(eid[:, 0:1], layer_base).then_inc(hn_ready.sem, 1)
                for tt in range(TT):
                    routing_halves(0, tt)
                    routing_pairs(0, tt)
                    routing_experts(0, tt)
                    publish(L, 0, tt)
                query_rest(L, 1)
                with dve.Fori(0, PH - 2) as h:
                    peer_head(L, h, True, True)
                    dve.drain()
                peer_head(L, PH - 2, True, False)
                dve.drain()
                peer_head(L, PH - 1, False, False)
                dve.drain()
                TS(layer_base, layer_base, float(EXPERTS), None, ALU.add)
                dve.drain()
            dve.wait_ge(gnat_in.sem, gnat_in.at(depth, 16))
            V.tensor_copy(eid[:, 0:1], layer_base)
            norm(x, root_ready.at(depth, 1), gain=gnat)


def constants():
    c = np.zeros((P, NCONST), np.float32)

    def put(name, v):
        c[:, CCOLS[name][0]:CCOLS[name][1]] = v
    i = np.arange(P)
    put("ident", np.eye(P))
    put("later", i[:, None] > i[None, :])
    put("upto", i[:, None] <= i[None, :])
    dist = i[:, None] - np.arange(2 * P)[None, :] + P
    put("dist", np.where((dist >= 0) & (dist < P), dist, FAR))
    put("time", np.arange(SEQ)[None, :])
    put("iota", np.arange(16)[None, :])
    return c


def lay_out(a, depth):
    f = lambda n: np.asarray(a[n])[:depth]
    w_in = f("w_in")
    L = depth

    def tiles(w):
        l, k, n = w.shape
        return w.reshape(l, k // P, P, n // P, P).transpose(0, 3, 2, 1, 4)

    def by_tiles(w, per):
        t = tiles(w)
        l, n, p, k, c = t.shape
        return t.reshape(l, n // per, per, p, k * c).transpose(0, 1, 3, 2, 4).reshape(l, n // per, P, UNIT)

    def by_rows(w, kts, cols):
        l, k, n = w.shape
        t = w.reshape(l, k // (kts * P), kts, P, n // cols, cols).transpose(0, 4, 1, 3, 2, 5)
        return t.reshape(l, -1, P, UNIT)

    q = w_in[:, :, 0:512].reshape(L, D, KVH, REP, HD).transpose(0, 1, 3, 2, 4).reshape(L, D, 512)
    k, v = w_in[:, :, 512:640], w_in[:, :, 640:768]
    u, z, xbc = w_in[:, :, 768:1280], w_in[:, :, 1280:2304], w_in[:, :, 2304:3584]
    wdt, gat = w_in[:, :, 3584:3600], w_in[:, :, 3600:6672]
    wao = f("w_attn_out").reshape(L, KVH, REP, HD, D).transpose(0, 2, 1, 3, 4).reshape(L, 512, D)
    wkv = f("xa_wkv")
    glu = np.stack([by_tiles(f("s5_glu_b"), 2), by_tiles(f("s5_glu_a"), 2)], 2).reshape(L, -1, P, UNIT)
    units = np.concatenate([
        by_tiles(np.concatenate([q, k, v, u, xbc], 2), 1), by_tiles(wkv[:, :, :256], 1), by_rows(wkv[:, :, 256:], 4, 256),
        by_rows(z, 2, 512), by_tiles(gat[:, :, :2 * D], 1), by_tiles(wao, 2), by_tiles(gat[:, :, 2 * D:], 1), glu,
        by_tiles(f("w_ssd_out"), 1), by_rows(f("w_o"), 2, 512), by_tiles(f("xa_wq"), 1), by_rows(f("xa_wo"), 2, 512),
    ], 1)
    assert units.shape[1] == UNITS
    units = np.concatenate([units.reshape(L * UNITS, P, UNIT), np.zeros((RING, P, UNIT), np.float32)])
    wq = f("peer_wq")
    wq = wq.reshape(L, KT, P, PH, 256).transpose(0, 3, 2, 1, 4).reshape(L * PH, P, 2 * UNIT)

    par = np.zeros((L + 1, P, NPAR), np.float32)

    def put(name, val):
        par[:L, :, COLS[name][0]:COLS[name][1]] = val.reshape(L, -1, COLS[name][1] - COLS[name][0])

    def states(t):
        r = t.reshape((L, 16, P) + t.shape[3:])
        return np.moveaxis(r, 1, 2)

    def chans(t):
        return t.reshape(L, -1, P).transpose(0, 2, 1)
    put("lr", states(f("s5_lambda_re")))
    put("li", states(f("s5_lambda_im")))
    put("ldt", states(np.repeat(f("s5_log_dt")[:, :, None], 64, 2)))
    put("bre", states(f("s5_b_re")))
    put("bim", states(f("s5_b_im")))
    put("cre", states(f("s5_c_re").transpose(0, 1, 3, 2)))
    put("cim", states(f("s5_c_im").transpose(0, 1, 3, 2)))
    put("s5d", chans(f("s5_d")))
    put("convw", f("ssd_conv_w").reshape(L, 4, 10, P).transpose(0, 3, 2, 1))
    put("convb", chans(f("ssd_conv_b")))
    for n, s in (("g_mix", "norm_mix"), ("g_x", "norm_xattn"), ("g_mem", "norm_mem"), ("g_ssd", "ssd_norm")):
        put(n, chans(f(s)))
    for n, s in (("dtb", "ssd_dt_bias"), ("alog", "ssd_a_log"), ("ssdd", "ssd_d"), ("sinks", "attn_sinks")):
        put(n, np.repeat(f(s)[:, None, :], P, 1))
    put("wdt", wdt.reshape(L, KT, P, 16).transpose(0, 2, 1, 3))
    put("k1", f("peer_k1").transpose(0, 2, 1))
    put("k2", f("peer_k2").transpose(0, 2, 1))
    table = np.concatenate([f("peer_u"), f("peer_v")], 2).reshape(L * EXPERTS, ROW)
    return {"x": np.asarray(a["x"]), "mem": np.asarray(a["mem"]), "units": units, "wq": wq, "par": par,
            "const": constants(), "g_ffn": f("norm_ffn"), "g_final": np.asarray(a["norm_final"]), "table": table}


def program(nc, arrays, depth):
    aps = [nc.dram_tensor(f"in_{n}", v.shape, F32, kind="ExternalInput").ap() for n, v in arrays.items()]
    out = nc.dram_tensor("out", (1, SEQ, D), F32, kind="ExternalOutput").ap()
    memT_d = nc.dram_tensor("memT_scratch", (P, KT * SEQ), F32, kind="Internal").ap()
    build(nc, depth, *aps, memT_d, out)


def kernel(**inputs):
    import concourse.bacc as bacc
    from concourse.bass_utils import run_bass_kernel_spmd

    depth = inputs["norm_mix"].shape[0]
    arrays = {k: np.ascontiguousarray(v) for k, v in lay_out(inputs, depth).items()}
    nc = bacc.Bacc("TRN2", target_bir_lowering=False, num_devices=1)
    program(nc, arrays, depth)
    r = run_bass_kernel_spmd(nc, [{f"in_{k}": v for k, v in arrays.items()}], core_ids=[0])
    return r.results[0]["out"]
```
